# Optimizing a Trainium2 kernel written in Bass

```python
import jax, jax.numpy as jnp
from jax import lax
import numpy as np
import math

D_MODEL = 2048
BATCH = 1
SEQ = 256
DEPTH = 1

POOL_WIDTH = D_MODEL // 2
POOL_WINDOWS = (2, 4, 8, 16)
N_POOL_GROUPS = len(POOL_WINDOWS)
POOL_GROUP = POOL_WIDTH // N_POOL_GROUPS
N_Q_HEADS = 16
N_KV_HEADS = 4
GROUP = N_Q_HEADS // N_KV_HEADS
HEAD_DIM = D_MODEL // N_Q_HEADS
NSA_WIDTH = N_Q_HEADS * HEAD_DIM
KV_WIDTH = N_KV_HEADS * HEAD_DIM
CMP_BLOCK = 32
CMP_STRIDE = 16
CMP_HIDDEN = 2 * HEAD_DIM
SEL_BLOCK = 64
N_SEL = 16
WINDOW = 512
Q_BLOCK = 128
ROPE_THETA = 10000.0
EPS = 1e-6
NEG = -1e30
FORCE = 1e6
N_BRANCHES = 2
IN_SPLITS = (POOL_WIDTH, POOL_WIDTH, NSA_WIDTH, KV_WIDTH, KV_WIDTH, KV_WIDTH, KV_WIDTH,
             KV_WIDTH, KV_WIDTH, NSA_WIDTH, 3 * N_Q_HEADS)
D_IN = sum(IN_SPLITS)


def rmsnorm(x, w):
    xf = x.astype(jnp.float32)
    y = xf * lax.rsqrt(jnp.mean(xf * xf, axis=-1, keepdims=True) + EPS)
    return (y * w.astype(jnp.float32)).astype(x.dtype)

def rope(x, pos):
    half = HEAD_DIM // 2
    inv = ROPE_THETA ** (-jnp.arange(half, dtype=jnp.float32) / half)
    ang = pos.astype(jnp.float32)[:, None] * inv[None, :]
    cos = jnp.cos(ang)[None, :, None, :]
    sin = jnp.sin(ang)[None, :, None, :]
    xf = x.astype(jnp.float32)
    x1, x2 = xf[..., :half], xf[..., half:]
    return jnp.concatenate([x1 * cos - x2 * sin, x2 * cos + x1 * sin], axis=-1).astype(x.dtype)

def pool_mixer(u, mix, scale):
    b, s, _ = u.shape
    ug = u.reshape(b, s, N_POOL_GROUPS, POOL_GROUP)
    uf = ug.astype(jnp.float32)
    c = jnp.pad(jnp.cumsum(uf, axis=1), ((0, 0), (1, 0), (0, 0), (0, 0)))
    t = np.arange(s)
    win = np.array(POOL_WINDOWS)
    lo = np.maximum(t[:, None] + 1 - win[None, :], 0)
    cnt = jnp.asarray(np.minimum(t[:, None] + 1, win[None, :]).astype(np.float32))
    c_lo = c[:, lo, np.arange(N_POOL_GROUPS)[None, :]]
    mean = (c[:, 1:] - c_lo) / cnt[None, :, :, None]
    pooled = (mean - uf).astype(u.dtype)
    z = jnp.einsum("bsgc,gcd->bsgd", pooled, mix).reshape(b, s, POOL_WIDTH)
    return z * scale

def compress(kraw, pe, w1, w2):
    s = kraw.shape[1]
    n_cmp = (s - CMP_BLOCK) // CMP_STRIDE + 1
    idx = np.arange(n_cmp)[:, None] * CMP_STRIDE + np.arange(CMP_BLOCK)[None, :]
    kb = kraw[:, idx] + pe[None, None, :, None, :]
    hdn = jax.nn.silu(jnp.einsum("bnlhd,ldf->bnhf", kb, w1))
    return jnp.einsum("bnhf,fe->bnhe", hdn, w2)

def nsa_attention(q, kc, vc, ks, vs, kw, vw, gates):
    b, s = q.shape[0], q.shape[1]
    n_cmp = kc.shape[1]
    n_blk = s // SEL_BLOCK
    n_sel = min(N_SEL, n_blk)
    scale = HEAD_DIM ** -0.5
    cmp_end = jnp.arange(n_cmp) * CMP_STRIDE + CMP_BLOCK - 1
    ratio = SEL_BLOCK // CMP_STRIDE
    sub = CMP_BLOCK // CMP_STRIDE
    sel_idx = (np.arange(n_blk)[:, None, None] * ratio + np.arange(ratio)[None, :, None]
               - np.arange(sub)[None, None, :]).reshape(n_blk, ratio * sub)
    sel_valid = jnp.asarray((sel_idx >= 0) & (sel_idx < n_cmp))
    sel_idx = np.clip(sel_idx, 0, n_cmp - 1)
    ks_blk = ks.reshape(b, n_blk, SEL_BLOCK, N_KV_HEADS, HEAD_DIM).transpose(0, 3, 1, 2, 4)
    vs_blk = vs.reshape(b, n_blk, SEL_BLOCK, N_KV_HEADS, HEAD_DIM).transpose(0, 3, 1, 2, 4)
    kw_pad = jnp.pad(kw, ((0, 0), (WINDOW, 0), (0, 0), (0, 0)))
    vw_pad = jnp.pad(vw, ((0, 0), (WINDOW, 0), (0, 0), (0, 0)))
    gather = jax.vmap(jax.vmap(lambda kt, ix: kt[ix]))
    jblk = jnp.arange(n_blk)

    def block(i):
        s0 = i * Q_BLOCK
        qb = lax.dynamic_slice_in_dim(q, s0, Q_BLOCK, axis=1)
        gb = lax.dynamic_slice_in_dim(gates, s0, Q_BLOCK, axis=1)
        tpos = s0 + jnp.arange(Q_BLOCK)
        sc = jnp.einsum("bqhgd,bnhd->bhgqn", qb, kc, preferred_element_type=jnp.float32) * scale
        cvalid = cmp_end[None, :] <= tpos[:, None]
        p_c = jnp.where(cvalid, jax.nn.softmax(jnp.where(cvalid, sc, NEG), axis=-1), 0.0)
        o_c = jnp.einsum("bhgqn,bnhe->bqhge", p_c.astype(vc.dtype), vc)
        imp_c = p_c.sum(axis=2)
        imp = jnp.where(sel_valid, imp_c[..., sel_idx], 0.0).sum(-1)
        jt = (tpos // SEL_BLOCK)[:, None]
        forced = (jblk[None, :] == 0) | (jblk[None, :] == jt) | (jblk[None, :] == jt - 1)
        imp = jnp.where(forced, FORCE, imp)
        imp = jnp.where(jblk[None, :] > jt, NEG, imp)
        _, top = lax.top_k(imp, n_sel)
        kg = gather(ks_blk, top)
        vg = gather(vs_blk, top)
        kpos = top[..., None] * SEL_BLOCK + jnp.arange(SEL_BLOCK)
        svalid = kpos <= tpos[None, None, :, None, None]
        ss = jnp.einsum("bqhgd,bhqnld->bhgqnl", qb, kg, preferred_element_type=jnp.float32) * scale
        ss = jnp.where(svalid[:, :, None], ss, NEG)
        p_s = jax.nn.softmax(ss.reshape(ss.shape[:4] + (-1,)), axis=-1).reshape(ss.shape)
        o_s = jnp.einsum("bhgqnl,bhqnle->bqhge", p_s.astype(vg.dtype), vg)
        kwb = lax.dynamic_slice_in_dim(kw_pad, s0, WINDOW + Q_BLOCK, axis=1)
        vwb = lax.dynamic_slice_in_dim(vw_pad, s0, WINDOW + Q_BLOCK, axis=1)
        wpos = s0 - WINDOW + jnp.arange(WINDOW + Q_BLOCK)
        diff = tpos[:, None] - wpos[None, :]
        wvalid = (diff >= 0) & (diff < WINDOW) & (wpos[None, :] >= 0)
        sw = jnp.einsum("bqhgd,bkhd->bhgqk", qb, kwb, preferred_element_type=jnp.float32) * scale
        p_w = jax.nn.softmax(jnp.where(wvalid, sw, NEG), axis=-1)
        o_w = jnp.einsum("bhgqk,bkhe->bqhge", p_w.astype(vwb.dtype), vwb)
        return gb[..., 0:1] * o_c + gb[..., 1:2] * o_s + gb[..., 2:3] * o_w

    out = lax.map(block, jnp.arange(s // Q_BLOCK))
    return out.transpose(1, 0, 2, 3, 4, 5).reshape(b, s, NSA_WIDTH)

def first_inputs(seed: int = 0) -> dict:
    key = jax.random.key(seed)
    ks = jax.random.split(key, 20)
    f32 = jnp.float32
    nrm = lambda k, shape, fan: jax.random.normal(k, shape, f32) * (fan ** -0.5)
    L = DEPTH
    return {
        "x": jax.random.normal(ks[0], (BATCH, SEQ, D_MODEL), f32),
        "norm_w": 1.0 + 0.05 * jax.random.normal(ks[1], (L, D_MODEL), f32),
        "w_in": nrm(ks[2], (L, D_MODEL, D_IN), D_MODEL),
        "pool_mix": nrm(ks[3], (L, N_POOL_GROUPS, POOL_GROUP, POOL_GROUP), POOL_GROUP),
        "pool_scale": 1.0 + 0.1 * jax.random.normal(ks[4], (L, POOL_WIDTH), f32),
        "cmp_pe_k": 0.1 * jax.random.normal(ks[5], (L, CMP_BLOCK, HEAD_DIM), f32),
        "cmp_w1_k": nrm(ks[6], (L, CMP_BLOCK, HEAD_DIM, CMP_HIDDEN), CMP_BLOCK * HEAD_DIM),
        "cmp_w2_k": nrm(ks[7], (L, CMP_HIDDEN, HEAD_DIM), CMP_HIDDEN),
        "cmp_pe_v": 0.1 * jax.random.normal(ks[8], (L, CMP_BLOCK, HEAD_DIM), f32),
        "cmp_w1_v": nrm(ks[9], (L, CMP_BLOCK, HEAD_DIM, CMP_HIDDEN), CMP_BLOCK * HEAD_DIM),
        "cmp_w2_v": nrm(ks[10], (L, CMP_HIDDEN, HEAD_DIM), CMP_HIDDEN),
        "w_pool_out": nrm(ks[11], (L, POOL_WIDTH, D_MODEL), POOL_WIDTH),
        "w_nsa_out": nrm(ks[12], (L, NSA_WIDTH, D_MODEL), NSA_WIDTH),
        "w_merge": nrm(ks[13], (L, D_MODEL, N_BRANCHES * D_MODEL), D_MODEL),
        "b_merge": 0.01 * jax.random.normal(ks[14], (L, N_BRANCHES * D_MODEL), f32),
        "w_out": nrm(ks[15], (L, D_MODEL, D_MODEL), D_MODEL),
        "final_norm_w": 1.0 + 0.05 * jax.random.normal(ks[16], (D_MODEL,), f32),
    }

def first_block(x, norm_w, w_in, pool_mix, pool_scale, cmp_pe_k, cmp_w1_k, cmp_w2_k,
              cmp_pe_v, cmp_w1_v, cmp_w2_v, w_pool_out, w_nsa_out, w_merge, b_merge,
              w_out, final_norm_w):
    b, s, _ = x.shape
    pos = jnp.arange(s)
    n_cmp = (s - CMP_BLOCK) // CMP_STRIDE + 1
    cmp_pos = jnp.arange(n_cmp) * CMP_STRIDE + CMP_BLOCK - 1
    split_at = np.cumsum(IN_SPLITS)[:-1].tolist()
    for layer in range(DEPTH):
        h = rmsnorm(x, norm_w[layer])
        proj = h @ w_in[layer]
        (u_pool, g_pool, q, kc_raw, vc_raw, k_sel, v_sel, k_win, v_win,
         g_nsa, g_br) = jnp.split(proj, split_at, axis=-1)
        y_pool = pool_mixer(u_pool, pool_mix[layer], pool_scale[layer]) * jax.nn.silu(g_pool)
        y_a = y_pool @ w_pool_out[layer]
        heads = lambda t, n: t.reshape(b, s, n, HEAD_DIM)
        qh = rope(heads(q, N_Q_HEADS), pos).reshape(b, s, N_KV_HEADS, GROUP, HEAD_DIM)
        kc = rope(compress(heads(kc_raw, N_KV_HEADS), cmp_pe_k[layer], cmp_w1_k[layer],
                           cmp_w2_k[layer]), cmp_pos)
        vc = compress(heads(vc_raw, N_KV_HEADS), cmp_pe_v[layer], cmp_w1_v[layer], cmp_w2_v[layer])
        ksh = rope(heads(k_sel, N_KV_HEADS), pos)
        kwh = rope(heads(k_win, N_KV_HEADS), pos)
        gates = jax.nn.sigmoid(g_br).reshape(b, s, N_KV_HEADS, GROUP, 3)
        o_nsa = nsa_attention(qh, kc, vc, ksh, heads(v_sel, N_KV_HEADS), kwh,
                              heads(v_win, N_KV_HEADS), gates)
        y_b = (o_nsa * jax.nn.silu(g_nsa)) @ w_nsa_out[layer]
        gm = jax.nn.sigmoid(h @ w_merge[layer] + b_merge[layer]).reshape(b, s, N_BRANCHES, D_MODEL)
        merged = gm[:, :, 0] * y_a + gm[:, :, 1] * y_b
        x = x + merged @ w_out[layer]
    return rmsnorm(x, final_norm_w)


CHUNK = 64
N_MEM = 256
N_BRANCH = 3
D_CONV = D_MODEL // 2
CONV_WIDTH = 31
ATTN_HEAD_DIM = 64
D_ATTN = D_MODEL // 2
N_ATTN_HEADS = D_ATTN // ATTN_HEAD_DIM
LEFT_CHUNKS = 8
BAND = LEFT_CHUNKS + 1
MAX_REL = 256
N_MEM_HEADS = 4
D_MEM = D_MODEL // 2
MEM_HEAD_DIM = D_MEM // N_MEM_HEADS
D_FF = ((8 * D_MODEL // 3 + 255) // 256) * 256
FFN_CONV_WIDTH = 3
D_IN_2 = 2 * D_CONV + 3 * D_ATTN + D_MEM + N_BRANCH * D_MODEL
SPLITS = (2 * D_CONV, 2 * D_CONV + 3 * D_ATTN, 2 * D_CONV + 3 * D_ATTN + D_MEM)
NEG_INF = -1e30


def rmsnorm_2(x, g):
    xf = x.astype(jnp.float32)
    y = xf * lax.rsqrt(jnp.mean(xf * xf, axis=-1, keepdims=True) + EPS)
    return (y * g.astype(jnp.float32)).astype(x.dtype)

def layernorm(x, g, b):
    xf = x.astype(jnp.float32)
    mu = jnp.mean(xf, axis=-1, keepdims=True)
    var = jnp.mean(jnp.square(xf - mu), axis=-1, keepdims=True)
    y = (xf - mu) * lax.rsqrt(var + EPS)
    return (y * g.astype(jnp.float32) + b.astype(jnp.float32)).astype(x.dtype)

def causal_dwconv(x, w, b):
    width = w.shape[0]
    ch = x.shape[-1]
    y = lax.conv_general_dilated(
        x, w[:, None, :].astype(x.dtype), window_strides=(1,),
        padding=[(width - 1, 0)], dimension_numbers=('NWC', 'WIO', 'NWC'),
        feature_group_count=ch)
    return y + b.astype(x.dtype)

def conv_module(u, conv_w, conv_b, ln_g, ln_b):
    a, gt = jnp.split(u, 2, axis=-1)
    h = a * jax.nn.sigmoid(gt)
    h = causal_dwconv(h, conv_w, conv_b)
    return jax.nn.silu(layernorm(h, ln_g, ln_b))

def chunk_attention(q, k, v, rel_bias):
    b, s, h, hd = q.shape
    nc = s // CHUNK
    qc = q.reshape(b, nc, CHUNK, h, hd)
    pad = ((0, 0), (LEFT_CHUNKS, 0), (0, 0), (0, 0), (0, 0))
    kp = jnp.pad(k.reshape(b, nc, CHUNK, h, hd), pad)
    vp = jnp.pad(v.reshape(b, nc, CHUNK, h, hd), pad)
    band_idx = jnp.arange(nc)[:, None] + jnp.arange(BAND)[None, :]
    kb = kp[:, band_idx].reshape(b, nc, BAND * CHUNK, h, hd)
    vb = vp[:, band_idx].reshape(b, nc, BAND * CHUNK, h, hd)
    scores = jnp.einsum('bcqhd,bckhd->bhcqk', qc, kb).astype(jnp.float32) * (hd ** -0.5)
    qi = jnp.arange(CHUNK)[:, None]
    km = jnp.arange(BAND * CHUNK)[None, :]
    dist = LEFT_CHUNKS * CHUNK + qi - km
    rel_idx = jnp.clip(dist, -MAX_REL, MAX_REL) + MAX_REL
    bias = rel_bias.astype(jnp.float32)[:, rel_idx]
    valid = jnp.repeat(band_idx >= LEFT_CHUNKS, CHUNK, axis=1)
    scores = scores + bias[None, :, None, :, :]
    scores = jnp.where(valid[None, None, :, None, :], scores, NEG_INF)
    p = jax.nn.softmax(scores, axis=-1).astype(v.dtype)
    out = jnp.einsum('bhcqk,bckhd->bcqhd', p, vb)
    return out.reshape(b, s, h * hd)

def memory_attention(q, km, vm):
    b, s, h, hd = q.shape
    scores = jnp.einsum('bshd,bmhd->bhsm', q, km).astype(jnp.float32) * (hd ** -0.5)
    p = jax.nn.softmax(scores, axis=-1).astype(vm.dtype)
    out = jnp.einsum('bhsm,bmhd->bshd', p, vm)
    return out.reshape(b, s, h * hd)

def second_inputs(seed: int = 0) -> dict:
    key = jax.random.key(seed)
    ks = jax.random.split(key, 24)

    def nrm(k, shape, scale):
        return jax.random.normal(k, shape, jnp.float32) * scale

    def gain(k, shape):
        return 1.0 + 0.05 * jax.random.normal(k, shape, jnp.float32)

    L = DEPTH
    return {
        'x': nrm(ks[0], (BATCH, SEQ, D_MODEL), 1.0),
        'mem': nrm(ks[1], (BATCH, N_MEM, D_MODEL), 1.0),
        'mix_norm_g': gain(ks[2], (L, D_MODEL)),
        'mem_norm_g': gain(ks[3], (L, D_MODEL)),
        'w_in': nrm(ks[4], (L, D_MODEL, D_IN_2), D_MODEL ** -0.5),
        'gate_b': nrm(ks[5], (L, N_BRANCH * D_MODEL), 0.1),
        'conv_w': nrm(ks[6], (L, CONV_WIDTH, D_CONV), CONV_WIDTH ** -0.5),
        'conv_b': nrm(ks[7], (L, D_CONV), 0.02),
        'conv_ln_g': gain(ks[8], (L, D_CONV)),
        'conv_ln_b': nrm(ks[9], (L, D_CONV), 0.02),
        'w_conv_out': nrm(ks[10], (L, D_CONV, D_MODEL), D_CONV ** -0.5),
        'rel_bias': nrm(ks[11], (L, N_ATTN_HEADS, 2 * MAX_REL + 1), 0.1),
        'w_attn_out': nrm(ks[12], (L, D_ATTN, D_MODEL), D_ATTN ** -0.5),
        'w_mem_kv': nrm(ks[13], (L, D_MODEL, 2 * D_MEM), D_MODEL ** -0.5),
        'w_mem_out': nrm(ks[14], (L, D_MEM, D_MODEL), D_MEM ** -0.5),
        'w_o': nrm(ks[15], (L, D_MODEL, D_MODEL), D_MODEL ** -0.5),
        'ffn_norm_g': gain(ks[16], (L, D_MODEL)),
        'w_up': nrm(ks[17], (L, D_MODEL, 2 * D_FF), D_MODEL ** -0.5),
        'ffn_conv_w': nrm(ks[18], (L, FFN_CONV_WIDTH, 2 * D_FF), FFN_CONV_WIDTH ** -0.5),
        'ffn_conv_b': nrm(ks[19], (L, 2 * D_FF), 0.02),
        'w_down': nrm(ks[20], (L, D_FF, D_MODEL), D_FF ** -0.5),
        'final_norm_g': gain(ks[21], (D_MODEL,)),
    }

def second_block(x, mem, mix_norm_g, mem_norm_g, w_in, gate_b, conv_w, conv_b, conv_ln_g, conv_ln_b,
              w_conv_out, rel_bias, w_attn_out, w_mem_kv, w_mem_out, w_o, ffn_norm_g, w_up,
              ffn_conv_w, ffn_conv_b, w_down, final_norm_g):
    b, s, d = x.shape
    h = x
    for l in range(DEPTH):
        xn = rmsnorm_2(h, mix_norm_g[l])
        proj = xn @ w_in[l]
        u_conv, qkv, q_mem, gates = jnp.split(proj, SPLITS, axis=-1)
        y_conv = conv_module(u_conv, conv_w[l], conv_b[l], conv_ln_g[l], conv_ln_b[l]) @ w_conv_out[l]
        q, k, v = jnp.split(qkv.reshape(b, s, 3, N_ATTN_HEADS, ATTN_HEAD_DIM), 3, axis=2)
        y_attn = chunk_attention(q[:, :, 0], k[:, :, 0], v[:, :, 0], rel_bias[l]) @ w_attn_out[l]
        mn = rmsnorm_2(mem, mem_norm_g[l])
        kv = (mn @ w_mem_kv[l]).reshape(b, mem.shape[1], 2, N_MEM_HEADS, MEM_HEAD_DIM)
        qm = q_mem.reshape(b, s, N_MEM_HEADS, MEM_HEAD_DIM)
        y_mem = memory_attention(qm, kv[:, :, 0], kv[:, :, 1]) @ w_mem_out[l]
        g = jax.nn.sigmoid(gates + gate_b[l]).reshape(b, s, N_BRANCH, d)
        merged = g[:, :, 0] * y_conv + g[:, :, 1] * y_attn + g[:, :, 2] * y_mem
        h = h + merged @ w_o[l]
        hn = rmsnorm_2(h, ffn_norm_g[l])
        up = causal_dwconv(hn @ w_up[l], ffn_conv_w[l], ffn_conv_b[l])
        val, gt = jnp.split(up, 2, axis=-1)
        h = h + (jax.nn.silu(gt) * val) @ w_down[l]
    return rmsnorm_2(h, final_norm_g)


def setup_inputs(seed=0):
    out = dict(first_inputs(seed))
    for name, value in second_inputs(seed + 1).items():
        if name != "x":
            out[name + "_2"] = value
    return out


def reference(
    x, norm_w, w_in, pool_mix, pool_scale, cmp_pe_k, cmp_w1_k, cmp_w2_k, cmp_pe_v, cmp_w1_v,
    cmp_w2_v, w_pool_out, w_nsa_out, w_merge, b_merge, w_out, final_norm_w, mem_2, mix_norm_g_2,
    mem_norm_g_2, w_in_2, gate_b_2, conv_w_2, conv_b_2, conv_ln_g_2, conv_ln_b_2, w_conv_out_2,
    rel_bias_2, w_attn_out_2, w_mem_kv_2, w_mem_out_2, w_o_2, ffn_norm_g_2, w_up_2,
    ffn_conv_w_2, ffn_conv_b_2, w_down_2, final_norm_g_2,
):
    x = first_block(
        x, norm_w, w_in, pool_mix, pool_scale, cmp_pe_k, cmp_w1_k, cmp_w2_k, cmp_pe_v, cmp_w1_v,
        cmp_w2_v, w_pool_out, w_nsa_out, w_merge, b_merge, w_out, final_norm_w,
    )
    return second_block(
        x, mem_2, mix_norm_g_2, mem_norm_g_2, w_in_2, gate_b_2, conv_w_2, conv_b_2, conv_ln_g_2,
        conv_ln_b_2, w_conv_out_2, rel_bias_2, w_attn_out_2, w_mem_kv_2, w_mem_out_2, w_o_2,
        ffn_norm_g_2, w_up_2, ffn_conv_w_2, ffn_conv_b_2, w_down_2, final_norm_g_2,
    )


_drawn_inputs = setup_inputs


def setup_inputs(seed=0):
    import zlib

    import numpy as np

    out = dict(_drawn_inputs(seed))
    spreads = {}
    factors = {'cmp_pe_k': 8.0,
     'cmp_w1_k': 2.922,
     'cmp_w2_k': 2.794,
     'cmp_pe_v': 6.514,
     'b_merge': 8.0,
     'mem_norm_g_2': 8.0,
     'gate_b_2': 4.125,
     'conv_b_2': 14.578,
     'conv_ln_b_2': 29.385,
     'rel_bias_2': 25.253,
     'ffn_conv_b_2': 11.954,
     'conv_ln_g_2': 8.0,
     'ffn_norm_g_2': 4.615}
    for name, (base, spread) in spreads.items():
        noise = np.random.default_rng([zlib.crc32(name.encode()), seed]).standard_normal(out[name].shape)
        drawn = base * np.exp(spread * noise) if base else spread * noise
        out[name] = __import__('jax').numpy.asarray(drawn.astype(out[name].dtype))
    for name, factor in factors.items():
        out[name] = (out[name] * factor).astype(out[name].dtype)
    return out
```

```python
from contextlib import ExitStack

import numpy as np

import concourse.bass as bass
from concourse import mybir

F32 = mybir.dt.float32
F32R = mybir.dt.float32r
ALU = mybir.AluOpType
ACT = mybir.ActivationFunctionType
AX = mybir.AxisListType

P = 128
T = 256
D = 2048
KD = D // P
POOL_WIDTH = 1024
HEADS, KV_HEADS, HEAD_DIM = 16, 4, 128
KV_WIDTH = KV_HEADS * HEAD_DIM
CMP_BLOCK, CMP_STRIDE = 32, 16
N_CMP = (T - CMP_BLOCK) // CMP_STRIDE + 1
N_BLOCKS = KV_HEADS * N_CMP
N_GATES = 3 * HEADS
EPS = 1e-6
NEG = -1e30
D_CONV, CONV_WIDTH = 1024, 31
D_ATTN, A_HEADS, A_DIM, CHUNK, MAX_REL = 1024, 16, 64, 64, 256
N_MEM, M_HEADS, M_DIM = 256, 4, 256
D_FF = 5632
FFN_TAPS = 3
UNIT = 256
TILE_K = 8

C_UPOOL = 0
C_GPOOL = C_UPOOL + POOL_WIDTH
C_Q = C_GPOOL + POOL_WIDTH
C_KC = C_Q + D
C_VC = C_KC + KV_WIDTH
C_KS = C_VC + KV_WIDTH
C_VS = C_KS + KV_WIDTH
C_KW = C_VS + KV_WIDTH
C_VW = C_KW + KV_WIDTH
C_GNSA = C_VW + KV_WIDTH
C_GBR = C_GNSA + D
C2_A = 0
C2_G = D_CONV
C2_Q = 2 * D_CONV
C2_K = C2_Q + D_ATTN
C2_V = C2_K + D_ATTN
C2_QM = C2_V + D_ATTN
C2_GATES = C2_QM + D_ATTN

VECS = [("norm_w", 16), ("pool_scale", 8), ("b_merge", 32), ("final_norm_w", 16), ("pe_k", 32),
        ("pe_v", 32), ("mix_norm", 16), ("mem_norm", 16), ("gate_b", 48), ("conv_w", 8 * CONV_WIDTH),
        ("conv_b", 8), ("ln_g", 8), ("ln_b", 8), ("ffn_norm", 16), ("ffn_w", 88 * FFN_TAPS),
        ("ffn_b", 88), ("final_norm_2", 16)]
VEC_AT = {}
NVEC = 0
for _name, _n in VECS:
    VEC_AT[_name] = (NVEC, _n)
    NVEC += _n

CONSTS = [("ident", P), ("ones", P), ("eps", 1), ("pad", 7), ("cos", T), ("sin", T), ("cos_c", 16), ("sin_c", 16),
          ("mask1", 512), ("mask0", 288), ("rowvalid", 2), ("rcnt", 64)]
CONST_AT = {}
NCONST = 0
for _name, _n in CONSTS:
    CONST_AT[_name] = (NCONST, _n)
    NCONST += _n


def shape_constants():
    c = np.zeros((P, NCONST), np.float32)

    def put(name, v):
        at, n = CONST_AT[name]
        c[:v.shape[0], at:at + v.shape[1]] = v

    half = HEAD_DIM // 2
    inv = np.float32(10000.0) ** (-np.arange(half, dtype=np.float32) / np.float32(half))
    inv = inv.astype(np.float32)

    def tables(pos):
        ang = (pos.astype(np.float32)[None, :] * inv[:, None]).astype(np.float32)
        co, si = np.cos(ang).astype(np.float32), np.sin(ang).astype(np.float32)
        return np.concatenate([co, co]), np.concatenate([-si, si])

    put("ident", np.eye(P, dtype=np.float32))
    put("ones", np.ones((P, P), np.float32))
    co, si = tables(np.arange(T))
    put("cos", co)
    put("sin", si)
    co, si = tables(np.arange(16) * CMP_STRIDE + CMP_BLOCK - 1)
    put("cos_c", co)
    put("sin_c", si)
    q = np.arange(P)[:, None]
    causal = np.where(np.arange(P)[None, :] <= q, 0.0, NEG).astype(np.float32)
    later = np.concatenate([np.zeros((P, P), np.float32), causal], 1)
    put("mask1", np.concatenate([later, later], 1))

    def cmp_mask(q0):
        n = np.arange(16)[None, :]
        ok = (n * CMP_STRIDE + CMP_BLOCK - 1 <= q0 + q) & (n < N_CMP)
        return np.where(ok, 0.0, NEG).astype(np.float32)

    put("mask0", np.concatenate([causal, causal, cmp_mask(0), cmp_mask(P)], 1))
    put("rowvalid", np.concatenate([q >= CMP_BLOCK - 1, q + P >= CMP_BLOCK - 1], 1).astype(np.float32))
    r = np.zeros((P, 4, 16), np.float32)
    for g, w in enumerate((2, 4, 8, 16)):
        r[:, g, :] = 1.0 / np.minimum(np.arange(16) + 1, w)
    put("rcnt", r.reshape(P, 64))
    put("eps", np.full((P, 1), EPS, np.float32))
    return c


class Queue:

    def __init__(self, sem):
        self.sem, self.count, self.steps, self.seen = sem, 0, [], {}

    def wait(self, *tokens):
        for sem, value in tokens:
            if value > self.seen.get(sem.name, 0):
                self.seen[sem.name] = value
                self.steps.append((sem, value))

    def run(self, fn, *tokens):
        self.wait(*tokens)
        self.count += 1
        self.steps.append(lambda e: fn(e).then_inc(self.sem, 1))
        return self.sem, self.count

    def dma(self, out, in_, sem_count, *tokens):
        self.wait(*tokens)
        sem_count[1] += 16
        sem = sem_count[0]
        self.steps.append(lambda e: e.dma_start(out, in_).then_inc(sem, 16))
        return sem, sem_count[1]

    def play(self, e):
        for s in self.steps:
            if isinstance(s, tuple):
                e.wait_ge(*s)
            else:
                s(e)


def two_blocks(nc, A, out):
    with ExitStack() as ctx:
        def sem(name):
            return ctx.enter_context(nc.semaphore(name))

        pe, act, dve, pool, sp = (Queue(sem(n)) for n in ("pe_done", "act_done", "dve_done", "pool_done", "sp_done"))

        KB = 1024
        ARENA = 207 * KB
        arena = ctx.enter_context(nc.sbuf_tensor("arena", [P, ARENA // 4], F32))
        base = nc.sbuf_base - ARENA
        names = [0]

        def at(name, kb, shape, dt=F32):
            names[0] += 1
            size = 4 * int(np.prod(shape[1:]))
            assert kb * KB + size <= ARENA, (name, kb, size)
            return nc.alloc_sbuf_tensor_at(f"{name}_{names[0]}", shape, dt, offset=base + int(kb * KB)).ap()

        RAW, HI, LO = 3, 3, 3
        raw = [at("w_raw", 8 * i, [P, TILE_K * UNIT]) for i in range(RAW)]
        w_hi = [at("w_hi", 24 + 8 * i, [P, TILE_K * UNIT], F32R) for i in range(HI)]
        w_lo = [at("w_lo", 48 + 8 * i, [P, TILE_K * UNIT], F32R) for i in range(LO)]
        RB, RA, RC, RD, RX = 72, 104, 136, 152, 168
        FREE1, FREE2 = 168, 184
        vecs = at("vecs", 195.5, [P, NVEC])
        consts = at("consts", 199.5, [P, NCONST])
        stats = at("stats", 206.25, [P, 128])

        def vec(name, i):
            a, _ = VEC_AT[name]
            return vecs[:, a + i:a + i + 1]

        def const(name, p0=0, p1=P):
            a, n = CONST_AT[name]
            return consts[p0:p1, a:a + n]

        ident, ones = const("ident"), const("ones")

        banks = [ctx.enter_context(nc.psum_tensor(f"bank{i}", [P, 512], F32)) for i in range(8)]
        main = banks[:3]
        SA, SB, TA, TB, OB = banks[3:8]

        d_vec, d_const = [sem("d_vec"), 0], [sem("d_const"), 0]
        d_x = [[sem(f"d_x{i}"), 0] for i in range(2)]
        t_vec = act.dma(vecs, A["vecs"], d_vec)
        t_const = act.dma(consts, A["consts"], d_const)

        d_raw = [[sem(f"d_raw{i}"), 0] for i in range(RAW)]
        tiles = []
        raw_free = [[] for _ in range(RAW)]
        hl_free = [None] * HI
        ready = []
        loaded = []

        def load_tile():
            i = len(loaded)
            src = tiles[i]
            nk, n = src.shape[1], src.shape[2]
            dst = raw[i % RAW][:, 0:nk * n].rearrange("p (k n) -> p k n", n=n)
            loaded.append((dst, sp.dma(dst, src, d_raw[i % RAW], *raw_free[i % RAW])))

        def split_tile():
            i = len(ready)
            while len(loaded) < min(i + RAW, len(tiles)):
                load_tile()
            src, t_load = loaded[i]
            nk, n = src.shape[1], src.shape[2]
            hi = w_hi[i % HI][:, 0:nk * n].rearrange("p (k n) -> p k n", n=n)
            lo = w_lo[i % LO][:, 0:nk * n].rearrange("p (k n) -> p k n", n=n)
            free = [hl_free[i % HI]] if hl_free[i % HI] else []
            t_hi = act.run(lambda e: e.activation(hi, src, ACT.Copy), t_load, *free)
            t_lo = dve.run(lambda e: e.tensor_tensor(lo, src, hi.bitcast(F32), ALU.subtract), t_hi, t_load, *free)
            raw_free[i % RAW] = [t_hi, t_lo]
            ready.append((hi, lo, t_hi, t_lo))
            if len(loaded) < len(tiles):
                load_tile()

        class Split:

            def __init__(self, name, kb_hi, kb_lo, nk, n=T, pad=0):
                self.flat_hi = at(name + "_hi", kb_hi, [P, nk * n + pad], F32R)
                self.flat_lo = at(name + "_lo", kb_lo, [P, nk * n + pad], F32R)
                self.hi, self.lo = (f[:, 0:nk * n].rearrange("p (k n) -> p k n", n=n) for f in (self.flat_hi, self.flat_lo))
                self.made = [None] * nk

            def make(self, k0, k1, src, *tokens):
                hi, lo = self.hi[:, k0:k1, :], self.lo[:, k0:k1, :]
                t_hi = act.run(lambda e: e.activation(hi, src, ACT.Copy), *tokens)
                t_lo = dve.run(lambda e: e.tensor_tensor(lo, src, hi.bitcast(F32), ALU.subtract), t_hi, *tokens)
                for k in range(k0, k1):
                    self.made[k] = (t_hi, t_lo)
                return t_hi, t_lo

        bank_free = {}

        def take(bank):
            return bank_free.get(bank.name, ())

        def give(bank, *tokens):
            bank_free[bank.name] = tokens

        def products(hi, lo, kk, moving, k, dst, cols, first):
            def fn(e):
                a = moving.hi[:, k, :]
                e.matmul(dst, hi[:, kk, cols], a, start=first, stop=True, skip_group_check=True)
                e.matmul(dst, hi[:, kk, cols], moving.lo[:, k, :], start=False, stop=True, skip_group_check=True)
                return e.matmul(dst, lo[:, kk, cols], a, start=False, stop=True, skip_group_check=True)
            return fn

        def products_token(hi, lo, kk, moving, k, dst, tok, n, first):
            def fn(e):
                a = moving.hi[:, k, tok]
                e.matmul(dst, a, hi[:, kk, 0:n], start=first, stop=True, skip_group_check=True)
                e.matmul(dst, a, lo[:, kk, 0:n], start=False, stop=True, skip_group_check=True)
                return e.matmul(dst, moving.lo[:, k, tok], hi[:, kk, 0:n], start=False, stop=True, skip_group_check=True)
            return fn

        def products_blocks(hi, lo, kk, moving, k, dst, first):
            def fn(e):
                a = slice(k * N_BLOCKS, k * N_BLOCKS + P)
                e.matmul(dst, moving.flat_hi[:, a], hi[:, kk, :], start=first, stop=True, skip_group_check=True)
                e.matmul(dst, moving.flat_hi[:, a], lo[:, kk, :], start=False, stop=True, skip_group_check=True)
                return e.matmul(dst, moving.flat_lo[:, a], hi[:, kk, :], start=False, stop=True, skip_group_check=True)
            return fn

        def products_narrow(slot, kk, moving, k, dst, first):
            def fn(e):
                a = slice(kk * N_GATES, kk * N_GATES + P)
                hi, lo, x = w_hi[slot % HI], w_lo[slot % LO], moving.hi[:, k, :]
                e.matmul(dst, hi[:, a], x, start=first, stop=True, skip_group_check=True)
                e.matmul(dst, hi[:, a], moving.lo[:, k, :], start=False, stop=True, skip_group_check=True)
                return e.matmul(dst, lo[:, a], x, start=False, stop=True, skip_group_check=True)
            return fn

        jobs = []
        side = []
        LOOK = 2

        def unit(w, rows, col, moving, evac, kind="channel", n=UNIT, before=None, after=None, k0=0, last_use=None):
            nk = (rows[1] - rows[0]) // P
            if kind == "narrow":
                view = w.rearrange("p (k n) -> p k n", n=n)
            else:
                view = w[rows[0]:rows[1], col:col + n].rearrange("(k p) n -> p k n", p=P)
            step = TILE_K if n == UNIT else nk
            parts = [(k, min(k + step, nk)) for k in range(0, nk, step)]
            for a, b in parts:
                tiles.append(view[:, a:b, :])
            jobs.append(dict(parts=parts, n=n, moving=moving, evac=evac, kind=kind, before=before, after=after, k0=k0,
                             last_use=last_use))

        def advance():
            for g in list(side):
                try:
                    next(g)
                except StopIteration:
                    side.remove(g)

        def later(n, g):
            for _ in range(n):
                yield
            return (yield from g)

        def finish(*gens):
            while any(g in side for g in gens):
                advance()

        def spawn(g):
            side.append(g)
            return g

        def drive():
            at_tile = 0
            for j, job in enumerate(jobs):
                if job["before"]:
                    job["before"]()
                bank = main[j % 3]
                n = job["n"]
                tok = None
                for a, b in job["parts"]:
                    while len(ready) < min(at_tile + 1 + LOOK, len(tiles)):
                        split_tile()
                    hi, lo, t_hi, t_lo = ready[at_tile]
                    pe.wait(t_hi, t_lo, *(take(bank) if a == 0 else ()))
                    mv = job["moving"]
                    outer = range(1) if job["kind"] in ("blocks", "narrow") else range(2)
                    for o in outer:
                        for kk in range(b - a):
                            k = job["k0"] + a + kk
                            first = a == 0 and o == 0 and kk == 0
                            pe.wait(*mv.made[k])
                            if job["kind"] == "channel":
                                f = products(hi, lo, kk, mv, k, bank[:, o * T:(o + 1) * T], slice(o * P, (o + 1) * P), first)
                            elif job["kind"] == "blocks":
                                pe.wait(*mv.made[min(k + 2, CMP_BLOCK - 1)])
                                f = products_blocks(hi, lo, kk, mv, k, bank[:, 0:T], first)
                            elif job["kind"] == "narrow":
                                f = products_narrow(at_tile, kk, mv, k, bank[:, 0:T], first)
                            else:
                                f = products_token(hi, lo, kk, mv, k, bank[:, o * T:o * T + n], slice(o * P, (o + 1) * P), n, first)
                            if o == outer[-1] and kk == b - a - 1:
                                tok = pe.run(f)
                            else:
                                pe.steps.append(f)
                    hl_free[at_tile % HI] = tok
                    at_tile += 1
                    if b < job["parts"][-1][1]:
                        advance()
                give(bank, *job["evac"](bank, tok))
                if job["after"]:
                    job["after"](tok)
                advance()
            while side:
                advance()

        sumsq = at("sumsq", 188, [P, T])
        rstd = at("rstd", 189, [P, T])
        sq = [at("sq", 184 + 2 * i, [P, 2, T]) for i in range(2)]
        sq_read = [(), ()]

        def last(q):
            return q.sem, q.count

        def column_sum(src, bank, *tokens):
            return pe.run(lambda e: e.matmul(bank[:, 0:T], ones, src, start=True, stop=True), t_const, *tokens, *take(bank))

        def inverse_std(t_sum, bank, n):
            eps = const("eps")
            t = act.run(lambda e: e.activation(rstd, bank[:, 0:T], ACT.Sqrt, bias=eps, scale=1.0 / n), t_sum, t_const, last(dve))
            give(bank, t)
            return dve.run(lambda e: e.reciprocal(rstd, rstd), t)

        def mean_square(src, tokens):
            for j in range(KD // 2):
                while len(tokens) <= j:
                    yield
                s, v = sq[j % 2], src[:, 2 * j:2 * j + 2, :]
                t_sq = act.run(lambda e, s=s, v=v: e.activation(s, v, ACT.Square), *tokens[j], *sq_read[j % 2])
                a, b = s[:, 0, :], s[:, 1, :]
                if j == 0:
                    t = dve.run(lambda e, a=a, b=b: e.tensor_tensor(sumsq, a, b, ALU.add), t_sq, last(pe))
                else:
                    t = dve.run(lambda e, a=a: e.tensor_tensor(sumsq, sumsq, a, ALU.add), t_sq, t)
                    t = dve.run(lambda e, b=b: e.tensor_tensor(sumsq, sumsq, b, ALU.add), t)
                sq_read[j % 2] = (t,)
                if j % 2:
                    yield
            t_sum = column_sum(sumsq, TB, t)
            yield
            return inverse_std(t_sum, TB, D)

        def rms_norm(src, tokens, gain, dst, split, *split_free):
            t_rstd = yield from mean_square(src, tokens)
            done = []
            for j in range(KD // 2):
                d = dst[:, 2 * j:2 * j + 2, :] if dst is not None else sq[j % 2]
                free = sq_read[j % 2] if dst is None else ()
                for c in range(2):
                    t = dve.run(lambda e, d=d, c=c, k=2 * j + c: e.scalar_tensor_tensor(
                        d[:, c, :], src[:, k, :], vec(gain, k), rstd, ALU.mult, ALU.mult), t_rstd, t_vec, *tokens[j], *free)
                if split is not None:
                    t_hl = split.make(2 * j, 2 * j + 2, d, t, *split_free)
                    if dst is None:
                        sq_read[j % 2] = t_hl
                done.append((t,))
                if j % 2:
                    yield
            return done

        xT, memT = A["x"], A["mem"]
        chunked = lambda ap: ap.rearrange("(k p) t -> p k t", p=P)
        x_sb = at("x", RC, [P, KD, T])
        h = Split("h", RA, RA + 16, KD)
        t_x = []
        for j in range(4):
            t_x += [[sp.dma(x_sb[:, 4 * j:4 * j + 4, :], chunked(xT)[:, 4 * j:4 * j + 4, :], [sem(f"d_xin{j}"), 0])]] * 2

        q1 = at("q", RB, [P, HEADS, T])
        k_sel = at("k_sel", RB + 16, [P, KV_HEADS, T])
        k_win = at("k_win", RB + 20, [P, KV_HEADS, T])
        v_sel = at("v_sel", RB + 24, [P, 2, KV_WIDTH])
        v_win = at("v_win", RB + 28, [P, 2, KV_WIDTH])
        raw_c = [at("kc_raw", RC, [P, KV_HEADS, T]), at("vc_raw", RC + 4, [P, KV_HEADS, T])]
        kb = at("kb", RC + 8, [P, CMP_BLOCK, KV_HEADS * N_CMP])
        kb_split = Split("kb", RD, RD + 8, CMP_BLOCK, N_BLOCKS, pad=P - N_BLOCKS)
        pad_from = CMP_BLOCK * N_BLOCKS
        evac_tmp = [at("evac_tmp", FREE1 + 2 * i, [P, 2, T]) for i in range(2)]
        s_buf = [at("scores", FREE1 + 4 + 3.125 * i, [P, 800]) for i in range(2)]
        pt_buf = at("pT", FREE1 + 10.25, [P, 1024])
        kc_t = at("kc", FREE1 + 14.25, [P, KV_HEADS, 16])
        gate6 = at("gate6", FREE1 + 14.5, [P, HEADS, 6])
        hid = at("hid", FREE1 + 14.875, [P, 2, KV_HEADS * N_CMP])
        vc_t = at("vc", FREE1 + 15.375, [16, KV_HEADS, HEAD_DIM])
        tmp_free = [(), ()]

        t_half = []

        def halve_biases():
            for name in ("b_merge", "gate_b"):
                a, n = VEC_AT[name]
                v = vecs[:, a:a + n]
                t_half.append(dve.run(lambda e, v=v: e.tensor_scalar(v, v, 0.5, None, ALU.mult), t_vec))

        halve_biases()

        rope_turn = [0]

        def rope_to(dst, note):
            def evac(bank, tok):
                i = rope_turn[0] % 2
                rope_turn[0] += 1
                sw = evac_tmp[i]
                z = bank[:, :].rearrange("p (c t) -> p c t", c=2)
                cos = const("cos").unsqueeze(1).broadcast_to([P, 2, T])
                sin = const("sin").unsqueeze(1).broadcast_to([P, 2, T])
                act.run(lambda e: e.copy(sw[0:64, :, :], z[64:128, :, :]), tok, *tmp_free[i])
                t_sw = act.run(lambda e: e.copy(sw[64:128, :, :], z[0:64, :, :]))
                t0 = dve.run(lambda e: e.tensor_tensor(dst, z, cos, ALU.mult), tok, t_sw, t_const)
                t1 = dve.run(lambda e: e.tensor_tensor(sw, sw, sin, ALU.mult), t_sw)
                t2 = dve.run(lambda e: e.tensor_tensor(dst, dst, sw, ALU.add), t0, t1)
                tmp_free[i] = (t2,)
                note.append(t2)
                return t_sw, t0
            return evac

        def to_sbuf(dst, scale=1.0, note=None):
            def evac(bank, tok):
                src = bank[:, :].rearrange("p (c t) -> p c t", c=2)
                t = act.run(lambda e: e.activation(dst, src, ACT.Copy, scale=scale), tok)
                if note is not None:
                    note.append(t)
                return (t,)
            return evac

        g_h = spawn(rms_norm(x_sb, t_x, "norm_w", None, h))

        def first_norm():
            for _ in range(4):
                advance()
            for _ in range(3):
                split_tile()
                advance()
            finish(g_h)

        w_in = A["w_in"]
        rows = (0, D)

        n_raw = [[], []]
        for s, col in enumerate((C_KC, C_VC)):
            for u in range(2):
                unit(w_in, rows, col + u * UNIT, h, to_sbuf(raw_c[s][:, 2 * u:2 * u + 2, :], note=n_raw[s]),
                     before=first_norm if s == 0 and u == 0 else None,
                 after=(lambda tok: start_blocks(0)) if s == 0 and u == 1 else None)
        n_k = []

        kb_free = [()]
        cmp_out = {}

        def blocks(s):
            name = ("pe_k", "pe_v")[s]
            kb4 = kb.rearrange("p l (h n) -> p l h n", h=KV_HEADS)
            t_kb = []
            for l in range(CMP_BLOCK):
                src = raw_c[s][:, :, l:l + CMP_STRIDE * (N_CMP - 1) + 1:CMP_STRIDE]
                t = pool.run(lambda e, l=l, src=src: e.tensor_scalar(kb4[:, l, :, :], src, vec(name, l), None, ALU.add),
                             *n_raw[s], t_vec, *kb_free[0])
                if l % 8 == 7:
                    t_kb.append(t)
            yield
            while s == 1 and "cmp0" not in cmp_out:
                yield
            for i in range(4):
                yield
                kb_free[0] = kb_split.make(8 * i, 8 * i + 8, kb[:, 8 * i:8 * i + 8, :], t_kb[i],
                                           *([cmp_out["cmp0"]] if s else []))
                yield

        pool.run(lambda e: e.memset(kb_split.flat_hi[:, pad_from:].bitcast(F32), 0.0))
        t_pad = pool.run(lambda e: e.memset(kb_split.flat_lo[:, pad_from:].bitcast(F32), 0.0))

        g_blocks = [None, None]

        def cmp_evac(s):
            def evac(bank, tok):
                z = bank[0:N_BLOCKS, 0:T]
                th = evac_tmp[0][0:N_BLOCKS, 0, :]
                t = act.run(lambda e: e.activation(th, z, ACT.Tanh, scale=0.5), tok, *tmp_free[0])
                t = dve.run(lambda e: e.scalar_tensor_tensor(hid_rows, th, 1.0, z, ALU.add, ALU.mult), t,
                            *((cmp_out["rows_read"],) if s else ()))
                tmp_free[0] = (t,)
                cmp_out["rows%d" % s] = t
                cmp_out["cmp%d" % s] = tok
                spawn(second_layer(s))
                return (t,)
            return evac

        w2_sb = [at("w2k", 190, [P, 2, HEAD_DIM]), at("w2v", 191, [P, 2, HEAD_DIM])]
        t_w2 = [act.dma(w2_sb[s], A["cmp_w2_" + "kv"[s]].rearrange("(k p) n -> p k n", p=P), [sem("d_w2" + "kv"[s]), 0])
                for s in range(2)]
        gate_rows = at("gate_rows", 193.5, [N_GATES, T])
        hid_rows = at("hid_rows", 192.5, [N_BLOCKS, T])
        kc_raw2 = at("kc2", 192, [P, KV_HEADS, N_CMP])
        kc_sw = at("kcsw", 192.25, [P, KV_HEADS, N_CMP])

        def second_layer(s):
            yield

            def turn(e):
                for f in range(2):
                    m = e.transpose(TA[:, f * 64:f * 64 + N_BLOCKS], hid_rows[:, f * P:(f + 1) * P],
                                    ident[0:N_BLOCKS, 0:N_BLOCKS])
                return m
            t = pe.run(turn, cmp_out["rows%d" % s], t_const, *take(TA))
            cmp_out["rows_read"] = t
            v = TA[:, 0:128].rearrange("p (f n) -> p f n", f=2)[:, :, 0:N_BLOCKS]
            t = act.run(lambda e: e.copy(hid, v), t, *((cmp_out["hid_read"],) if s else ()))
            give(TA, t)
            cmp_out["hid%d" % s] = t
            yield
            if s == 0:
                ps = TA[:, 0:KV_HEADS * N_CMP]

                def mm(e):
                    for f in range(2):
                        m = e.matmul(ps, w2_sb[0][:, f, :], hid[:, f, :], start=f == 0, stop=f == 1)
                    return m
                t = pe.run(mm, cmp_out["hid0"], t_w2[0], *take(TA))
                cmp_out["hid_read"] = t
                z = ps.rearrange("p (h n) -> p h n", h=KV_HEADS)
                shape = [P, KV_HEADS, N_CMP]
                cos = const("cos_c")[:, 0:N_CMP].unsqueeze(1).broadcast_to(shape)
                sin = const("sin_c")[:, 0:N_CMP].unsqueeze(1).broadcast_to(shape)
                yield
                t_z = dve.run(lambda e: e.memset(kc_t, 0.0))
                act.run(lambda e: e.activation(kc_sw[0:64], z[64:128], ACT.Copy, scale=0.5), t)
                t_sw = act.run(lambda e: e.activation(kc_sw[64:128], z[0:64], ACT.Copy, scale=0.5))
                t0 = dve.run(lambda e: e.scalar_tensor_tensor(kc_raw2, z, 0.5, cos, ALU.mult, ALU.mult), t, t_sw, t_const)
                t1 = dve.run(lambda e: e.tensor_tensor(kc_sw, kc_sw, sin, ALU.mult), t_sw)
                t2 = dve.run(lambda e: e.tensor_tensor(kc_t[:, :, 0:N_CMP], kc_raw2, kc_sw, ALU.add), t0, t1, t_z)
                give(TA, t_sw, t0)
                cmp_out["kc"] = t2
            else:
                def mm(e):
                    for hh in range(KV_HEADS):
                        for f in range(2):
                            m = e.matmul(TA[0:N_CMP, hh * P:(hh + 1) * P], hid[:, f, hh * N_CMP:(hh + 1) * N_CMP],
                                         w2_sb[1][:, f, :], start=f == 0, stop=f == 1)
                    return m
                t = pe.run(mm, cmp_out["hid1"], t_w2[1], *take(TA))
                yield
                t = act.run(lambda e: e.activation(vc_t[0:N_CMP], TA[0:N_CMP, :].rearrange("p (h n) -> p h n", h=KV_HEADS),
                                                   ACT.Copy, scale=0.5), t)
                give(TA, t)
                cmp_out["vc"] = t

        def start_blocks(s):
            g_blocks[s] = spawn(blocks(s))

        for u in range(2):
            unit(w_in, rows, C_KS + u * UNIT, h, rope_to(k_sel[:, 2 * u:2 * u + 2, :], n_k))
        for u in range(2):
            unit(w_in, rows, C_KW + u * UNIT, h, rope_to(k_win[:, 2 * u:2 * u + 2, :], n_k))

        def cmp_unit(s):
            w = A["cmp_w1_" + "kv"[s]].rearrange("l d f -> (l d) f")
            unit(w, (0, CMP_BLOCK * HEAD_DIM), 0, kb_split, cmp_evac(s), kind="blocks", before=lambda: (finish(g_blocks[s]), pe.wait(t_pad)))

        cmp_unit(0)
        jobs[-1]["after"] = lambda tok: start_blocks(1)
        for u in range(2):
            unit(w_in, rows, C_VS + u * UNIT, h, to_sbuf(v_sel[:, :, u * UNIT:(u + 1) * UNIT], note=n_k), kind="token")
        for u in range(2):
            unit(w_in, rows, C_VW + u * UNIT, h, to_sbuf(v_win[:, :, u * UNIT:(u + 1) * UNIT], note=n_k), kind="token")
        def gates_evac(bank, tok):
            th = gate_rows
            t_z = act.run(lambda e: e.activation(th, bank[0:N_GATES, 0:T], ACT.Tanh, scale=0.5), tok)
            t = dve.run(lambda e: e.tensor_scalar(th, th, 0.5, 0.5, ALU.mult, ALU.add), t_z)

            def turn(e):
                for qt in range(2):
                    m = e.transpose(TB[:, qt * 64:qt * 64 + N_GATES], th[:, qt * P:(qt + 1) * P], ident[0:N_GATES, 0:N_GATES])
                return m

            def place():
                yield
                t_t = pe.run(turn, t, t_const, *take(TB))
                yield
                g = lambda qt, br: TB[:, qt * 64:qt * 64 + N_GATES].rearrange("p (h b) -> p h b", b=3)[:, :, br]
                for i, (qt, br) in enumerate(((1, 1), (1, 2), (0, 1), (0, 2))):
                    dve.run(lambda e, i=i, v=g(qt, br): e.tensor_copy(gate6[:, :, i], v), t_t)
                rv = const("rowvalid")
                for i in range(2):
                    t_g = dve.run(lambda e, i=i, v=g(i, 0): e.tensor_scalar(gate6[:, :, 4 + i], v, rv[:, i:i + 1], None, ALU.mult))
                give(TB, t_g)
                cmp_out["gates"] = t_g

            spawn(place())
            return (t_z,)

        unit(A["w_gates"], rows, 0, h, gates_evac, kind="narrow", n=N_GATES)
        n_q = []
        for u in range(8):
            if u == 1:
                cmp_unit(1)
            unit(w_in, rows, C_Q + u * UNIT, h, rope_to(q1[:, 2 * u:2 * u + 2, :], n_q),
                 after=(lambda tok: spawn(attention1())) if u == 7 else None)

        SC1 = HEAD_DIM ** -0.5
        s_free, head_done = [(), ()], [None] * HEADS
        pt_free = [()]

        def head1(hd):
            kv, b = hd // (HEADS // KV_HEADS), hd % 2
            S = s_buf[b]
            st = stats[:, 16 * b:16 * b + 16]
            mx, sm = st[:, 0:6], st[:, 6:12]
            q0_, q1_ = q1[:, hd, 0:P], q1[:, hd, P:T]

            def score(e):
                e.matmul(SA[:, 0:T], q1_, k_sel[:, kv, :], start=True, stop=True)
                e.matmul(SA[:, T:2 * T], q1_, k_win[:, kv, :], start=True, stop=True)
                e.matmul(SB[:, 0:P], q0_, k_sel[:, kv, 0:P], start=True, stop=True)
                e.matmul(SB[:, P:2 * P], q0_, k_win[:, kv, 0:P], start=True, stop=True)
                e.matmul(SB[:, 256:272], q0_, kc_t[:, kv, :], start=True, stop=True)
                return e.matmul(SB[:, 272:288], q1_, kc_t[:, kv, :], start=True, stop=True)
            t_s = pe.run(score, n_q[hd // 2], *n_k, cmp_out["kc"], *take(SA), *take(SB))
            yield
            t_a = dve.run(lambda e: e.scalar_tensor_tensor(S[:, 0:512], SA[:, :], SC1, const("mask1"), ALU.mult, ALU.add),
                          t_s, *s_free[b])
            t_b = dve.run(lambda e: e.scalar_tensor_tensor(S[:, 512:800], SB[:, 0:288], SC1, const("mask0"), ALU.mult, ALU.add))
            give(SA, t_a)
            give(SB, t_b)
            segs = [(0, 256), (256, 256), (512, 128), (640, 128), (768, 16), (784, 16)]
            groups = [(0, 2, 256), (2, 2, 128), (4, 2, 16)]
            for i, m, n in groups:
                v = S[:, segs[i][0]:segs[i][0] + m * n].rearrange("p (m n) -> p m n", m=m)
                t_m = dve.run(lambda e, v=v, i=i, m=m: e.tensor_reduce(mx[:, i:i + m], v, AX.X, ALU.max), t_a, t_b)
            t_m = dve.run(lambda e: e.tensor_scalar(mx, mx, -1.0, None, ALU.mult), t_m)
            for i, (o, n) in enumerate(segs):
                v = S[:, o:o + n]
                t_e = act.run(lambda e, v=v, i=i: e.activation(v, v, ACT.Exp, bias=mx[:, i:i + 1], accum_out=sm[:, i:i + 1]), t_m)
            yield
            t = dve.run(lambda e: e.reciprocal(sm, sm), t_e)
            t = dve.run(lambda e: e.tensor_tensor(sm, sm, gate6[:, hd, :], ALU.mult), t, cmp_out["gates"])
            for i, m, n in groups:
                v = S[:, segs[i][0]:segs[i][0] + m * n].rearrange("p (m n) -> p m n", m=m)
                c = sm[:, i:i + m].unsqueeze(2).broadcast_to([P, m, n])
                t_p = dve.run(lambda e, v=v, c=c: e.tensor_tensor(v, v, c, ALU.mult), t)
            yield

            def flip(e):
                e.transpose(TA[:, 0:P], S[:, 512:640], ident)
                e.transpose(TA[:, P:2 * P], S[:, 0:P], ident)
                e.transpose(TA[:, 2 * P:3 * P], S[:, 640:768], ident)
                e.transpose(TA[:, 3 * P:4 * P], S[:, 256:384], ident)
                e.transpose(TB[:, 0:P], S[:, P:2 * P], ident)
                e.transpose(TB[:, P:2 * P], S[:, 384:512], ident)
                e.transpose(TB[0:16, 2 * P:3 * P], S[:, 768:784], ident)
                return e.transpose(TB[0:16, 3 * P:4 * P], S[:, 784:800], ident)
            t_t = pe.run(flip, t_p, *take(TA), *take(TB))
            s_free[b] = (t_t,)
            yield
            pt = pt_buf
            t0 = act.run(lambda e: e.copy(pt[:, 0:512], TA[:, :]), t_t, *pt_free[0])
            t1 = dve.run(lambda e: e.tensor_copy(pt[:, 512:768], TB[:, 0:256]), t_t, *pt_free[0])
            t2 = dve.run(lambda e: e.tensor_copy(pt[0:16, 768:1024], TB[0:16, 256:512]))
            give(TA, t0)
            give(TB, t1, t2)
            yield

            def values(e):
                c = slice(kv * P, (kv + 1) * P)
                e.matmul(OB[:, 0:T], v_sel[:, 0, c], pt[:, 0:256], start=True, stop=False, skip_group_check=True)
                e.matmul(OB[:, 0:T], v_win[:, 0, c], pt[:, 256:512], start=False, stop=False, skip_group_check=True)
                e.matmul(OB[:, 0:T], vc_t[0:N_CMP, kv, :], pt[0:N_CMP, 768:1024], start=False, stop=False, skip_group_check=True)
                e.matmul(OB[:, P:T], v_sel[:, 1, c], pt[:, 512:640], start=False, stop=False, skip_group_check=True)
                return e.matmul(OB[:, P:T], v_win[:, 1, c], pt[:, 640:768], start=False, stop=True, skip_group_check=True)
            t_v = pe.run(values, t0, t1, t2, *n_k, cmp_out["vc"], *take(OB))
            pt_free[0] = (t_v,)
            yield
            t_o = act.run(lambda e: e.copy(q1[:, hd, :], OB[:, 0:T]), t_v)
            give(OB, t_o)
            head_done[hd] = t_o

        def attention1():
            for hd in range(HEADS):
                g = spawn(head1(hd))
                next(g)
                for _ in range(3):
                    yield
        g_att1 = []

        pgate = at("pool_gate", RC, [P, 8, T])
        pu = at("pool_u", FREE1 + 17.375, [P, 2, T])
        pp = [at("pool_sum", FREE1 + 19.375 + 2 * i, [P, 2, T]) for i in range(2)]
        pooled = Split("pooled", FREE1 + 23.375, FREE1 + 25.375, 2)
        ypool = Split("ypool", RD, RD + 8, 8)
        pool_free = {"pu": (), "pp": (), "split": ()}
        n_pg = []

        def gpool_evac(j):
            def evac(bank, tok):
                th = evac_tmp[j % 2]
                z = bank[:, :].rearrange("p (c t) -> p c t", c=2)
                t = act.run(lambda e: e.activation(th, z, ACT.Tanh, scale=0.5), tok, *tmp_free[j % 2])
                t = dve.run(lambda e: e.scalar_tensor_tensor(pgate[:, 2 * j:2 * j + 2, :], th, 1.0, z, ALU.add, ALU.mult),
                            t, *kb_free[0], last(pool))
                tmp_free[j % 2] = (t,)
                n_pg.append(t)
                return (t,)
            return evac

        def upool_evac(g):
            def evac(bank, tok):
                w = 2 << g
                z = bank[:, :].rearrange("p (c t) -> p c t", c=2)
                t_u = act.run(lambda e: e.copy(pu, z), tok, *pool_free["pu"], cmp_out["vc"])
                src, t_prev = pu, t_u
                free = pool_free["pp"]
                for i in range(g + 1):
                    d = 1 << i
                    dst = pp[i % 2]
                    t0 = dve.run(lambda e, s=src, o=dst, d=d: e.tensor_tensor(o[:, :, d:], s[:, :, d:], s[:, :, :T - d], ALU.add),
                                 t_prev, *free)
                    t_prev = dve.run(lambda e, s=src, o=dst, d=d: e.tensor_copy(o[:, :, 0:d], s[:, :, 0:d]), t_prev, t0)
                    src = dst
                rc = const("rcnt")[:, 16 * g:16 * g + 16].unsqueeze(1).broadcast_to([P, 2, 16])
                ta = dve.run(lambda e, s=src: e.tensor_tensor(s[:, :, 0:16], s[:, :, 0:16], rc, ALU.mult), t_prev, t_const)
                tb = dve.run(lambda e, s=src: e.scalar_tensor_tensor(pu[:, :, 16:], s[:, :, 16:], 1.0 / w, pu[:, :, 16:],
                                                                     ALU.mult, ALU.subtract), t_prev)
                tc = dve.run(lambda e, s=src: e.tensor_tensor(pu[:, :, 0:16], s[:, :, 0:16], pu[:, :, 0:16], ALU.subtract), ta)
                t_hl = pooled.make(0, 2, pu, tb, tc, *pool_free["split"])
                pool_free["pu"] = t_hl
                pool_free["pp"] = (tc,)
                return (t_u,)
            return evac

        def mix_evac(g):
            def evac(bank, tok):
                pool_free["split"] = (tok,)
                y = pp[0]
                for c in range(2):
                    k = 2 * g + c
                    t = dve.run(lambda e, c=c, k=k: e.scalar_tensor_tensor(
                        y[:, c, :], bank[:, c * T:(c + 1) * T], vec("pool_scale", k), pgate[:, k, :], ALU.mult, ALU.mult),
                        tok, n_pg[g], *pool_free["pp"])
                t_hl = ypool.make(2 * g, 2 * g + 2, y, t, *kb_free[0], cmp_out["kb_read"])
                pool_free["pp"] = t_hl
                return (t,)
            return evac

        for j in range(4):
            unit(w_in, rows, C_GPOOL + j * UNIT, h, gpool_evac(j))
            if j >= 1:
                unit(A["pool_mix"][j - 1], (0, UNIT), 0, pooled, mix_evac(j - 1))
            unit(w_in, rows, C_UPOOL + j * UNIT, h, upool_evac(j),
                 before=(lambda: cmp_out.__setitem__("kb_read", last(pe))) if j == 0 else None)

        ma = at("merged_a", RC, [P, KD, T])
        gm1 = at("gate_b1", RD, [P, KD, T])
        gate_t = {}
        n_ma, n_gm1 = [], []

        def gate0_evac(c):
            def evac(bank, tok):
                th = evac_tmp[c % 2]
                for i in range(2):
                    t = act.run(lambda e, i=i: e.activation(th[:, i, :], bank[:, i * T:(i + 1) * T], ACT.Tanh,
                                                            bias=vec("b_merge", 2 * c + i), scale=0.5), tok, *t_half, *tmp_free[c % 2])
                gate_t[c] = t
                return (t,)
            return evac

        def ya_evac(c):
            def evac(bank, tok):
                th = evac_tmp[c % 2]
                z = bank[:, :].rearrange("p (c t) -> p c t", c=2)
                t = dve.run(lambda e: e.scalar_tensor_tensor(ma[:, 2 * c:2 * c + 2, :], th, 1.0, z, ALU.add, ALU.mult),
                            tok, gate_t[c], *ypool.made[7])
                tmp_free[c % 2] = (t,)
                n_ma.append(t)
                return (t,)
            return evac

        def ya_unit(c):
            unit(A["w_pool_out"], (0, POOL_WIDTH), c * UNIT, ypool, ya_evac(c),
                 after=(lambda tok: gate_t.__setitem__("ypool_read", tok)) if c == 7 else None)

        for c in range(8):
            unit(A["w_merge"], rows, c * UNIT, h, gate0_evac(c))
            if c == 0:
                unit(A["pool_mix"][3], (0, UNIT), 0, pooled, mix_evac(3))
            else:
                ya_unit(c - 1)
        ya_unit(7)

        def gate1_evac(c):
            def evac(bank, tok):
                for i in range(2):
                    t = act.run(lambda e, i=i: e.activation(gm1[:, 2 * c + i, :], bank[:, i * T:(i + 1) * T], ACT.Tanh,
                                                            bias=vec("b_merge", 16 + 2 * c + i), scale=0.5),
                                tok, *t_half, gate_t["ypool_read"])
                n_gm1.append(t)
                return (t,)
            return evac

        for c in range(8):
            unit(A["w_merge"], rows, D + c * UNIT, h, gate1_evac(c))

        n_o = []

        def gnsa_evac(c):
            def evac(bank, tok):
                th = evac_tmp[c % 2]
                z = bank[:, :].rearrange("p (c t) -> p c t", c=2)
                o = q1[:, 2 * c:2 * c + 2, :]
                t = act.run(lambda e: e.activation(th, z, ACT.Tanh, scale=0.5), tok, *tmp_free[c % 2])
                t_z = dve.run(lambda e: e.scalar_tensor_tensor(th, th, 1.0, z, ALU.add, ALU.mult), t)
                t = dve.run(lambda e: e.tensor_tensor(o, o, th, ALU.mult), t_z, head_done[2 * c], head_done[2 * c + 1])
                tmp_free[c % 2] = (t,)
                n_o.append(t)
                return (t_z,)
            return evac

        def wait_heads(c):
            def f():
                while head_done[2 * c + 1] is None:
                    advance()
            return f

        o_split = Split("o", RA, RA + 16, KD)

        def split_o(tok):
            for c in range(8):
                o_split.make(2 * c, 2 * c + 2, q1[:, 2 * c:2 * c + 2, :], n_o[c], tok)

        for c in range(8):
            unit(w_in, rows, C_GNSA + c * UNIT, h, gnsa_evac(c), before=wait_heads(c),
                 after=split_o if c == 7 else None)

        merged = Split("merged", RB, RB + 16, KD)
        xr = [at("x_again", FREE1 + 8 + 2 * i, [P, 2, T]) for i in range(2)]
        mtmp = [at("merge_tmp", FREE1 + 4 + 2 * i, [P, 2, T]) for i in range(2)]
        mtmp_free = [(), ()]

        def yb_evac(c):
            def evac(bank, tok):
                m = mtmp[c % 2]
                z = bank[:, :].rearrange("p (c t) -> p c t", c=2)
                t_z = dve.run(lambda e: e.scalar_tensor_tensor(m, gm1[:, 2 * c:2 * c + 2, :], 1.0, z, ALU.add, ALU.mult),
                              tok, n_gm1[c], *mtmp_free[c % 2], *s_free[0], *s_free[1])
                t = dve.run(lambda e: e.tensor_tensor(m, m, ma[:, 2 * c:2 * c + 2, :], ALU.add), t_z, n_ma[c])
                mtmp_free[c % 2] = merged.make(2 * c, 2 * c + 2, m, t, *o_split.made[15], *pt_free[0], head_done[15])
                return (t_z,)
            return evac

        for c in range(8):
            unit(A["w_nsa_out"], rows, c * UNIT, o_split, yb_evac(c))

        mem_sb = at("mem", RC, [P, KD, T])
        mn = Split("mn", RA, RA + 16, KD)
        d_mem = [sem("d_mem"), 0]
        g_mem = [None]

        def start_mem(tok):
            t = act.dma(mem_sb, chunked(memT), d_mem, last(dve), tok)
            g_norms[0] = spawn(norms_between())
            g_mem[0] = spawn(later(3, rms_norm(mem_sb, [[t]] * 8, "mem_norm", None, mn, tok)))
        jobs[-1]["after"] = start_mem

        x1 = at("x1", RD, [P, KD, T])
        t_xr = {}
        n_x1, x1_tokens = [], []

        def load_x(c):
            def f():
                t_xr[c] = act.dma(xr[c % 2], chunked(xT)[:, 2 * c:2 * c + 2, :], d_x[c % 2],
                                  *([n_x1[c - 2]] if c >= 2 else [last(pe)]))
            return f

        def wout_evac(c):
            def evac(bank, tok):
                z = bank[:, :].rearrange("p (c t) -> p c t", c=2)
                t = dve.run(lambda e: e.scalar_tensor_tensor(x1[:, 2 * c:2 * c + 2, :], z, 0.25, xr[c % 2], ALU.mult, ALU.add),
                            tok, t_xr[c], *merged.made[15])
                n_x1.append(t)
                x1_tokens.append((t,))
                return (t,)
            return evac

        for c in range(8):
            unit(A["w_out"], rows, c * UNIT, merged, wout_evac(c), before=load_x(c))

        x2_dram = nc.dram_tensor("x2_scratch", (P, KD * T), F32).ap().rearrange("p (k t) -> p k t", k=KD)
        xn = Split("xn", RB, RB + 16, KD)
        k_mem = at("k_mem", RC, [P, 8, T])
        v_mem = at("v_mem", RC + 8, [P, 2, D_ATTN])
        n_km = []
        d_x2 = [sem("d_x2"), 0]

        def norms_between():
            while g_mem[0] in side:
                yield
            done = yield from rms_norm(x1, x1_tokens, "final_norm_w", x1, None)
            t_wout = b2["wout"]
            b2["x2"] = [act.dma(x2_dram, x1, d_x2, done[-1][0])]
            yield from rms_norm(x1, done, "mix_norm", None, xn, t_wout)
            b2["xn"] = xn.made[15]
            e2_free[:] = sq_read

        b2 = {}
        g_norms = [None]

        e2_free = [(), ()]

        def after_wout(tok):
            b2["wout"] = tok

        jobs[-1]["after"] = after_wout
        for u in range(4):
            unit(A["w_mem_kv"], rows, u * UNIT, mn,
                 to_sbuf(k_mem[:, 2 * u:2 * u + 2, :], note=n_km), before=(lambda: finish(g_mem[0])) if u == 0 else None)
        for u in range(4):
            unit(A["w_mem_kv"], rows, D_ATTN + u * UNIT, mn,
                 to_sbuf(v_mem[:, :, u * UNIT:(u + 1) * UNIT], note=n_km), kind="token",
                 after=(lambda tok: b2.__setitem__("mn_read", tok)) if u == 3 else None)

        PAD = CONV_WIDTH - 1
        w_in2 = A["w_in_2"]
        glu = at("glu", RD, [P, 8, PAD + T])
        cy = at("conv_y", RA + 24, [P, 8, T])
        yc = Split("yc", RX, RX + 8, 8)
        e2 = sq

        def a_evac(j):
            def evac(bank, tok):
                z = bank[:, :].rearrange("p (c t) -> p c t", c=2)
                if j == 0:
                    b2["pad"] = pool.run(lambda e: e.memset(glu[:, :, 0:PAD], 0.0), *b2["x2"], *b2["xn"])
                t = act.run(lambda e: e.activation(a_buf, z, ACT.Copy, scale=0.5), tok,
                            *((b2["glu"],) if "glu" in b2 else b2["xn"]))
                b2["a"] = t
                return (t,)
            return evac

        a_buf = at("glu_a", 190, [P, 2, T])

        def g_evac(j):
            def evac(bank, tok):
                th = e2[j % 2]
                z = bank[:, :].rearrange("p (c t) -> p c t", c=2)
                t = act.run(lambda e: e.activation(th, z, ACT.Tanh, scale=0.5), tok, *e2_free[j % 2])
                t = dve.run(lambda e: e.scalar_tensor_tensor(glu[:, 2 * j:2 * j + 2, PAD:], th, 1.0, a_buf, ALU.add, ALU.mult),
                            t, b2["a"], *b2["x2"], *b2["xn"])
                e2_free[j % 2] = (t,)
                b2["glu"] = t
                conv_ready.append(t)
                return (b2["a"], t)
            return evac

        conv_ready = []
        TAPS_A_SLOT = 8

        def conv():
            n = 0
            for j in range(4):
                while len(conv_ready) <= j:
                    yield
                last_t = [None, None]
                for c in range(2):
                    k = 2 * j + c
                    last_t[c] = act.run(lambda e, k=k: e.activation(cy[:, k, :], glu[:, k, 0:T], ACT.Identity,
                                                                    bias=vec("conv_b", k), scale=vec("conv_w", k * CONV_WIDTH)),
                                        conv_ready[j], b2["pad"], b2["mn_read"])
                for tap in range(1, CONV_WIDTH):
                    for c in range(2):
                        k = 2 * j + c
                        last_t[c] = dve.run(lambda e, k=k, tap=tap: e.scalar_tensor_tensor(
                            cy[:, k, :], glu[:, k, tap:tap + T], vec("conv_w", k * CONV_WIDTH + tap), cy[:, k, :],
                            ALU.mult, ALU.add), last_t[c])
                        n += 1
                        if n % TAPS_A_SLOT == 0:
                            yield
                b2["conv"] = last_t[0], last_t[1]
            yield
            by_t = cy.rearrange("p k t -> p t k")
            t = dve.run(lambda e: e.tensor_reduce(sumsq, by_t, AX.X, ALU.add), *b2["conv"], last(pe))
            t = column_sum(sumsq, TB, t)
            yield
            mean = TB[:, 0:T].unsqueeze(1).broadcast_to([P, 4, T])
            for g in range(2):
                t_c = dve.run(lambda e, g=g: e.scalar_tensor_tensor(cy[:, 4 * g:4 * g + 4, :], mean, -1.0 / D_CONV,
                                                                    cy[:, 4 * g:4 * g + 4, :], ALU.mult, ALU.add), t)
            give(TB, t_c)
            sqv = glu[:, :, 0:T]
            t = act.run(lambda e: e.activation(sqv, cy, ACT.Square), t_c)
            yield
            by_t2 = sqv.rearrange("p k t -> p t k")
            t = dve.run(lambda e: e.tensor_reduce(sumsq, by_t2, AX.X, ALU.add), t, last(pe))
            t = column_sum(sumsq, TB, t)
            b2["glu_read"] = (last(dve),)
            yield
            t = inverse_std(t, TB, D_CONV)
            r = rstd.unsqueeze(1).broadcast_to([P, 4, T])
            for g in range(2):
                t_g = dve.run(lambda e, g=g: e.tensor_tensor(cy[:, 4 * g:4 * g + 4, :], cy[:, 4 * g:4 * g + 4, :], r, ALU.mult), t)
            yield
            for j in range(4):
                th = e2[j % 2]
                for c in range(2):
                    k = 2 * j + c
                    t = act.run(lambda e, k=k: e.activation(cy[:, k, :], cy[:, k, :], ACT.Identity, bias=vec("ln_b", k),
                                                            scale=vec("ln_g", k)), t_g)
                v = cy[:, 2 * j:2 * j + 2, :]
                t = act.run(lambda e, th=th, v=v: e.activation(th, v, ACT.Tanh, scale=0.5), t, *e2_free[j % 2])
                t = dve.run(lambda e, th=th, v=v: e.scalar_tensor_tensor(v, th, 1.0, v, ALU.add, ALU.mult), t)
                e2_free[j % 2] = (t,)
                t_hl = yc.make(2 * j, 2 * j + 2, v, t, b2["rx_free"])
                b2["cy_read"] = t_hl
                yield

        g_conv = [None]

        def start_conv(_):
            g_conv[0] = spawn(conv())
            b2["rx_free"] = last(pe)

        for j in range(4):
            unit(w_in2, rows, C2_A + j * UNIT, xn, a_evac(j), before=(lambda: finish(g_norms[0])) if j == 0 else None)
            unit(w_in2, rows, C2_G + j * UNIT, xn, g_evac(j), after=start_conv if j == 0 else None)

        q2 = at("q2", RA, [P, 8, T])
        k2 = at("k2", RA + 8, [P, 8, T])
        v2 = at("v2", RA + 16, [P, 2, D_ATTN])
        n_q2, n_k2, n_v2 = [], [], []

        def to_a(dst, note):
            def evac(bank, tok):
                src = bank[:, :].rearrange("p (c t) -> p c t", c=2)
                t = act.run(lambda e: e.copy(dst, src), tok, b2["mn_read"])
                note.append(t)
                return (t,)
            return evac

        for u in range(4):
            unit(w_in2, rows, C2_Q + u * UNIT, xn, to_a(q2[:, 2 * u:2 * u + 2, :], n_q2))
        for u in range(4):
            unit(w_in2, rows, C2_K + u * UNIT, xn, to_a(k2[:, 2 * u:2 * u + 2, :], n_k2))
        for u in range(4):
            unit(w_in2, rows, C2_V + u * UNIT, xn, to_a(v2[:, :, u * UNIT:(u + 1) * UNIT], n_v2), kind="token",
                 after=(lambda tok: spawn(attention2())) if u == 3 else None)

        SC2 = A_DIM ** -0.5
        spare = 199.5 + 264 * 4 / KB
        bias = [at("bias", 192, [P, T + P]), at("bias", spare, [P, T + P])]
        s2 = [at("scores2", 190, [P, T + P]), at("scores2", spare + 1.5, [P, T + P])]
        pt2 = [at("pT2", 193.5, [P, T + P]), at("pT2", spare + 3, [P, T + P])]
        s_mem = at("scores_mem", 190, [P, 2 * T])
        pt_mem = at("pT_mem", 193.5, [P, 2 * T])
        d_bias = [[sem(f"d_bias{i}"), 0] for i in range(2)]
        bias_free, s2_free, pt2_free = [(), ()], [(), ()], [(), ()]
        head2_done = [None] * A_HEADS
        def head2(hd):
            ch, r, b = hd // 2, 64 * (hd % 2), hd % 2
            st = stats[:, 16 * b:16 * b + 16]
            mx, sm = st[:, 0:2], st[:, 2:4]
            B, S, pt = bias[b], s2[b], pt2[b]
            parts = (slice(0, T), slice(T, T + P))
            t_b = pool.dma(B, A["rel_bias"][hd], d_bias[b], *bias_free[b], b2["glu"])
            pool.run(lambda e: e.memset(B[0:64, T - CHUNK:T], NEG), t_b)
            t_m = pool.run(lambda e: e.memset(B[0:64, T + P - CHUNK:T + P], NEG))
            yield

            def score(e):
                kk = slice(r, r + 64)
                e.matmul(SA[:, 0:T], q2[kk, ch, P:T], k2[kk, ch, :], start=True, stop=True)
                return e.matmul(SA[:, T:T + P], q2[kk, ch, 0:P], k2[kk, ch, 0:P], start=True, stop=True)
            t_s = pe.run(score, n_q2[-1], n_k2[-1], *take(SA))
            t = dve.run(lambda e: e.scalar_tensor_tensor(S, SA[:, 0:T + P], SC2, B, ALU.mult, ALU.add), t_s, t_m,
                        *s2_free[b], b2["glu"])
            give(SA, t)
            bias_free[b] = (t,)
            dve.run(lambda e: e.tensor_reduce(mx[:, 0:1], S[:, parts[0]], AX.X, ALU.max), t)
            t = dve.run(lambda e: e.tensor_reduce(mx[:, 1:2], S[:, parts[1]], AX.X, ALU.max))
            t = dve.run(lambda e: e.tensor_scalar(mx, mx, -1.0, None, ALU.mult), t)
            for i in range(2):
                t_e = act.run(lambda e, v=S[:, parts[i]], i=i: e.activation(v, v, ACT.Exp, bias=mx[:, i:i + 1],
                                                                            accum_out=sm[:, i:i + 1]), t)
            t = dve.run(lambda e: e.reciprocal(sm, sm), t_e)
            for i in range(2):
                t_p = dve.run(lambda e, v=S[:, parts[i]], i=i: e.tensor_scalar(v, v, sm[:, i:i + 1], None, ALU.mult), t)
            yield

            def flip(e):
                e.transpose(TA[:, 0:P], S[:, 256:384], ident)
                e.transpose(TA[:, P:2 * P], S[:, 0:P], ident)
                return e.transpose(TA[:, 2 * P:3 * P], S[:, P:T], ident)
            t_t = pe.run(flip, t_p, *take(TA))
            s2_free[b] = (t_t,)
            t_pt = act.run(lambda e: e.copy(pt, TA[:, 0:T + P]), t_t, *pt2_free[b])
            give(TA, t_pt)
            yield

            def values(e):
                c = slice(hd * A_DIM, (hd + 1) * A_DIM)
                e.matmul(OB[r:r + 64, 0:T], v2[:, 0, c], pt[:, 0:T], start=True, stop=False, skip_group_check=True)
                return e.matmul(OB[r:r + 64, P:T], v2[:, 1, c], pt[:, T:], start=False, stop=True, skip_group_check=True)
            t_v = pe.run(values, t_pt, n_v2[-1], *take(OB))
            pt2_free[b] = (t_v,)
            t_o = act.run(lambda e: e.copy(q2[r:r + 64, ch, :], OB[r:r + 64, 0:T]), t_v)
            give(OB, t_o)
            head2_done[hd] = t_o

        def attention2():
            for hd in range(A_HEADS):
                next(spawn(head2(hd)))
                yield

        m2 = at("merged2", RD, [P, KD, T])
        gtmp = [at("gate_tmp", 184 + 2 * i, [P, 2, T]) for i in range(2)]
        m2_split = Split("merged2", RA, RA + 16, KD)
        n_m2 = {}

        def gate_evac2(br, c):
            def evac(bank, tok):
                th = gtmp[c % 2]
                for i in range(2):
                    t = act.run(lambda e, i=i: e.activation(th[:, i, :], bank[:, i * T:(i + 1) * T], ACT.Tanh,
                                                            bias=vec("gate_b", 16 * br + 2 * c + i), scale=0.5),
                                tok, *t_half, *e2_free[c % 2])
                n_m2["g", br, c] = t
                return (t,)
            return evac

        def y_evac2(br, c):
            def evac(bank, tok):
                th = gtmp[c % 2]
                m = m2[:, 2 * c:2 * c + 2, :]
                z = bank[:, :].rearrange("p (c t) -> p c t", c=2)
                tg = n_m2["g", br, c]
                if br == 0:
                    t_z = t = dve.run(lambda e: e.scalar_tensor_tensor(m, th, 1.0, z, ALU.add, ALU.mult), tok, tg, *b2["glu_read"])
                else:
                    t_z = dve.run(lambda e: e.scalar_tensor_tensor(th, th, 1.0, z, ALU.add, ALU.mult), tok, tg)
                    t = dve.run(lambda e: e.scalar_tensor_tensor(m, m, 0.5 if br == 1 else 1.0, th, ALU.mult, ALU.add), t_z,
                                n_m2["m", br - 1, c])
                e2_free[c % 2] = (t,)
                n_m2["m", br, c] = t
                return (t_z,)
            return evac

        def branch(br, w, moving, first_before, last_after):
            for c in range(8):
                unit(w_in2, rows, C2_GATES + br * D + c * UNIT, xn, gate_evac2(br, c))
                unit(w, (0, 1024), c * UNIT, moving, y_evac2(br, c), before=first_before if c == 0 else None,
                     after=last_after if c == 7 else None)

        def conv_ready_for_use():
            finish(g_conv[0])

        branch(0, A["w_conv_out"], yc, conv_ready_for_use, lambda tok: b2.__setitem__("yc_read", tok))

        qm = at("q_mem", RA + 8, [P, 8, T])
        n_qm = []
        SCM = M_DIM ** -0.5

        def heads2_done():
            while head2_done[-1] is None:
                advance()

        def qm_evac(u):
            def evac(bank, tok):
                src = bank[:, :].rearrange("p (c t) -> p c t", c=2)
                t = act.run(lambda e: e.copy(qm[:, 2 * u:2 * u + 2, :], src), tok, head2_done[-1])
                n_qm.append(t)
                return (t,)
            return evac

        ao = Split("attn_out", RX, RX + 8, 8)
        mo = Split("mem_out", RA + 16, RA + 24, 8)

        def headm(m):
            yield
            c0 = 2 * m
            st = stats[:, 32 + 8 * (m % 2):40 + 8 * (m % 2)]
            mx, sm = st[:, 0:2], st[:, 2:4]
            S, pt = s_mem, pt_mem

            def score(e):
                for qt in range(2):
                    for i in range(2):
                        x = e.matmul(SA[:, qt * T:(qt + 1) * T], qm[:, c0 + i, qt * P:(qt + 1) * P], k_mem[:, c0 + i, :],
                                     start=i == 0, stop=i == 1)
                return x
            t_s = pe.run(score, n_qm[m], *n_km[0:4], *take(SA))
            v3 = SA[:, :].rearrange("p (m n) -> p m n", m=2)
            t = dve.run(lambda e: e.tensor_reduce(mx, v3, AX.X, ALU.max), t_s)
            t = dve.run(lambda e: e.tensor_scalar(mx, mx, -SCM, None, ALU.mult), t)
            for i in range(2):
                t_e = act.run(lambda e, i=i: e.activation(S[:, i * T:(i + 1) * T], SA[:, i * T:(i + 1) * T], ACT.Exp,
                                                          bias=mx[:, i:i + 1], scale=SCM, accum_out=sm[:, i:i + 1]),
                              t, *s2_free[0])
            give(SA, t_e)
            t = dve.run(lambda e: e.reciprocal(sm, sm), t_e)
            for i in range(2):
                t_p = dve.run(lambda e, i=i: e.tensor_scalar(S[:, i * T:(i + 1) * T], S[:, i * T:(i + 1) * T], sm[:, i:i + 1],
                                                             None, ALU.mult), t)
            yield

            def flip(e):
                for kt in range(2):
                    for qt in range(2):
                        x = e.transpose(TA[:, kt * T + qt * P:kt * T + (qt + 1) * P], S[:, qt * T + kt * P:qt * T + (kt + 1) * P], ident)
                return x
            t_t = pe.run(flip, t_p, *take(TA))
            s2_free[0] = (t_t,)
            t = act.run(lambda e: e.copy(pt, TA[:, :]), t_t, *pt2_free[0])
            give(TA, t)
            yield

            def values(e):
                for i in range(2):
                    for kt in range(2):
                        x = e.matmul(OB[:, i * T:(i + 1) * T], v_mem[:, kt, (c0 + i) * P:(c0 + i + 1) * P],
                                     pt[:, kt * T:(kt + 1) * T], start=kt == 0, stop=kt == 1)
                return x
            t_v = pe.run(values, t, *n_km[4:8], *take(OB))
            pt2_free[0] = (t_v,)
            v = OB[:, :].rearrange("p (c t) -> p c t", c=2)
            t_o = act.run(lambda e: e.copy(qm[:, c0:c0 + 2, :], v), t_v)
            give(OB, t_o)
            mo.make(c0, c0 + 2, qm[:, c0:c0 + 2, :], t_o, head2_done[-1], *b2["cy_read"])

        def mem_heads():
            for m in range(M_HEADS):
                yield from headm(m)

        def split_ao(tok):
            for c in range(4):
                ao.make(2 * c, 2 * c + 2, q2[:, 2 * c:2 * c + 2, :], head2_done[4 * c + 1], head2_done[4 * c + 3], b2["yc_read"])
            g_memh.append(spawn(mem_heads()))

        g_memh = []
        for u in range(4):
            unit(w_in2, rows, C2_QM + u * UNIT, xn, qm_evac(u), before=heads2_done if u == 0 else None,
                 after=split_ao if u == 3 else None)
        branch(1, A["w_attn_out"], ao, None, None)

        def mem_ready():
            finish(g_memh[0])

        def split_m2(tok):
            for c in range(8):
                m2_split.make(2 * c, 2 * c + 2, m2[:, 2 * c:2 * c + 2, :], n_m2["m", 2, c], tok)
            b2["m2_split"] = m2_split.made[15]

        branch(2, A["w_mem_out"], mo, mem_ready, split_m2)

        hres = at("h_res", RD, [P, KD, T])
        x2r = [at("x2_again", RX + 2 * i, [P, 2, T]) for i in range(2)]
        n_h, h_tokens, t_x2r = [], [], {}
        d_x2r = [[sem(f"d_x2r{i}"), 0] for i in range(2)]

        def load_x2(c):
            def f():
                t_x2r[c] = act.dma(x2r[c % 2], x2_dram[:, 2 * c:2 * c + 2, :], d_x2r[c % 2], *b2["x2"],
                                   *([n_h[c - 2]] if c >= 2 else [last(pe)]))
            return f

        def wo_evac(c):
            def evac(bank, tok):
                z = bank[:, :].rearrange("p (c t) -> p c t", c=2)
                t = dve.run(lambda e: e.scalar_tensor_tensor(hres[:, 2 * c:2 * c + 2, :], z, 0.5, x2r[c % 2], ALU.mult, ALU.add),
                            tok, t_x2r[c], *b2["m2_split"])
                n_h.append(t)
                h_tokens.append((t,))
                return (t,)
            return evac

        hn = Split("hn", RB, RB + 16, KD)
        g_ffn = [None]

        def after_wo(c):
            def f(tok):
                if c == 0:
                    g_ffn[0] = spawn(rms_norm(hres, h_tokens, "ffn_norm", None, hn, tok))
                b2["a_free"] = tok
            return f

        for c in range(8):
            unit(A["w_o"], rows, c * UNIT, m2_split, wo_evac(c), before=load_x2(c), after=after_wo(c))

        HALF = D_FF // 2
        HK = HALF // P
        gated = Split("gated", RA, RA + 22, HK)
        fv = [at("ffn_val", RX + 4 * i, [P, 2, T]) for i in range(2)]
        fg = [at("ffn_gate", RX + 2 + 4 * i, [P, 2, T]) for i in range(2)]
        ft = [at("ffn_tanh", RX + 8 + 2 * i, [P, 2, T]) for i in range(2)]
        f_free = {0: (), 1: ()}
        gated_free = [None]
        ffn = {}

        def conv3(dst, bank, tok, k0, *free):
            w = lambda i, tap: vec("ffn_w", (k0 + i) * FFN_TAPS + tap)
            z = lambda i, n: bank[:, i * T:i * T + n]
            for i in range(2):
                t = act.run(lambda e, i=i: e.activation(dst[:, i, :], z(i, T), ACT.Identity, bias=vec("ffn_b", k0 + i),
                                                        scale=w(i, 2)), tok, *free)
            last_t = [t, t]
            for back in (1, 2):
                for i in range(2):
                    last_t[i] = dve.run(lambda e, i=i, b=back: e.scalar_tensor_tensor(
                        dst[:, i, b:], z(i, T - b), w(i, 2 - b), dst[:, i, b:], ALU.mult, ALU.add), last_t[i])
            return last_t

        def val_evac(half, j):
            def evac(bank, tok):
                done = conv3(fv[j % 2], bank, tok, half * HK + 2 * j, *f_free[j % 2], b2["wo_x2"])
                ffn["v"] = done
                return tuple(done)
            return evac

        def gate_evac(half, j):
            def evac(bank, tok):
                b = j % 2
                done = conv3(fg[b], bank, tok, D_FF // P + half * HK + 2 * j, *f_free[b], b2["wo_x2"])
                t = act.run(lambda e: e.activation(ft[b], fg[b], ACT.Tanh, scale=0.5), *done, *f_free[b])
                t = dve.run(lambda e: e.scalar_tensor_tensor(fg[b], ft[b], 1.0, fg[b], ALU.add, ALU.mult), t)
                t = dve.run(lambda e: e.tensor_tensor(fg[b], fg[b], fv[b], ALU.mult), t, *ffn["v"])
                f_free[b] = gated.make(2 * j, 2 * j + 2, fg[b], t, gated_free[0], b2["a_free"])
                return tuple(done)
            return evac

        def down_evac(half, c):
            def evac(bank, tok):
                z = bank[:, :].rearrange("p (c t) -> p c t", c=2)
                m = hres[:, 2 * c:2 * c + 2, :]
                t = dve.run(lambda e: e.scalar_tensor_tensor(m, z, 0.5, m, ALU.mult, ALU.add), tok, n_h[c],
                            *([hn.made[15][1]] if half == 0 else []))
                n_h[c] = t
                return (t,)
            return evac

        def ffn_start():
            finish(g_ffn[0])
            b2["wo_x2"] = n_h[7]
            gated_free[0] = b2["a_free"]

        for half in range(2):
            for j in range(HALF // UNIT):
                unit(A["w_up"], rows, half * HALF + j * UNIT, hn, val_evac(half, j),
                     before=ffn_start if half == 0 and j == 0 else None)
                unit(A["w_up"], rows, D_FF + half * HALF + j * UNIT, hn, gate_evac(half, j))
            for c in range(8):
                unit(A["w_down"], (half * HALF, (half + 1) * HALF), c * UNIT, gated, down_evac(half, c),
                     after=(lambda tok: gated_free.__setitem__(0, tok)) if c == 7 else None)

        drive()

        final = []

        def last_norm():
            final.extend((yield from rms_norm(hres, [[t] for t in n_h], "final_norm_2", hres, None)))

        finish(spawn(last_norm()))
        d_out = [sem("d_out"), 0]
        out_v = chunked(out)
        for j in range(8):
            t_out = sp.dma(out_v[:, 2 * j:2 * j + 2, :], hres[:, 2 * j:2 * j + 2, :], d_out, *final[j])
        sp.wait(t_out)
        sp.wait(*b2["x2"])

        block = ctx.enter_context(nc.Block())

        @block.sync
        def _(e):
            sp.play(e)

        @block.scalar
        def _(e):
            act.play(e)

        @block.vector
        def _(e):
            dve.play(e)

        @block.gpsimd
        def _(e):
            pool.play(e)

        @block.tensor
        def _(e):
            pe.play(e)


def kernel(**inputs):
    import concourse.bacc as bacc
    from concourse.bass_utils import run_bass_kernel_spmd as run

    def layer(name):
        return np.ascontiguousarray(np.asarray(inputs[name])[0])

    def chunks(v):
        return v.reshape(-1, P).T

    def taps(w):
        return w.reshape(w.shape[0], -1, P).transpose(2, 1, 0).reshape(P, -1)

    parts = {
        "norm_w": chunks(layer("norm_w")), "pool_scale": chunks(layer("pool_scale")),
        "b_merge": chunks(layer("b_merge")), "final_norm_w": chunks(np.asarray(inputs["final_norm_w"])),
        "pe_k": layer("cmp_pe_k").T, "pe_v": layer("cmp_pe_v").T,
        "mix_norm": chunks(layer("mix_norm_g_2")), "mem_norm": chunks(layer("mem_norm_g_2")),
        "gate_b": chunks(layer("gate_b_2")), "conv_w": taps(layer("conv_w_2")), "conv_b": chunks(layer("conv_b_2")),
        "ln_g": chunks(layer("conv_ln_g_2")), "ln_b": chunks(layer("conv_ln_b_2")),
        "ffn_norm": chunks(layer("ffn_norm_g_2")), "ffn_w": taps(layer("ffn_conv_w_2")),
        "ffn_b": chunks(layer("ffn_conv_b_2")), "final_norm_2": chunks(np.asarray(inputs["final_norm_g_2"])),
    }
    windows = np.lib.stride_tricks.sliding_window_view(layer("rel_bias_2")[:, ::-1], T, axis=1)
    rows_q = windows[:, MAX_REL - np.arange(T), :]
    rel = np.concatenate([rows_q[:, P:, :], rows_q[:, :P, :P]], axis=2)
    w_gates = layer("w_in")[:, C_GBR:].reshape(KD, P, N_GATES).transpose(1, 0, 2).reshape(P, KD * N_GATES)
    arrays = {
        "vecs": np.concatenate([parts[name] for name, _ in VECS], axis=1), "consts": shape_constants(),
        "x": layer("x").T, "mem": layer("mem_2").T, "rel_bias": rel,
        "w_in": layer("w_in"), "w_gates": w_gates, "pool_mix": layer("pool_mix"), "cmp_w1_k": layer("cmp_w1_k"), "cmp_w2_k": layer("cmp_w2_k"),
        "cmp_w1_v": layer("cmp_w1_v"), "cmp_w2_v": layer("cmp_w2_v"), "w_pool_out": layer("w_pool_out"),
        "w_nsa_out": layer("w_nsa_out"), "w_merge": layer("w_merge"), "w_out": layer("w_out"),
        "w_in_2": layer("w_in_2"), "w_conv_out": layer("w_conv_out_2"), "w_attn_out": layer("w_attn_out_2"),
        "w_mem_kv": layer("w_mem_kv_2"), "w_mem_out": layer("w_mem_out_2"), "w_o": layer("w_o_2"),
        "w_up": layer("w_up_2"), "w_down": layer("w_down_2"),
    }
    arrays = {k: np.ascontiguousarray(v) for k, v in arrays.items()}
    nc = bacc.Bacc("TRN2", target_bir_lowering=False, num_devices=1)
    aps = {k: nc.dram_tensor(k, v.shape, F32, kind="ExternalInput").ap() for k, v in arrays.items()}
    out = nc.dram_tensor("out", (D, T), F32, kind="ExternalOutput").ap()
    two_blocks(nc, aps, out)
    got = run(nc, [arrays], core_ids=[0]).results[0]["out"]
    return np.ascontiguousarray(got.T)[None]
```

```python
from contextlib import ExitStack

import numpy as np

import concourse.bass as bass
from concourse import mybir

F32 = mybir.dt.float32
F32R = mybir.dt.float32r
ALU = mybir.AluOpType
ACT = mybir.ActivationFunctionType
AX = mybir.AxisListType

P = 128
T = 256
D = 2048
KD = D // P
POOL_WIDTH = 1024
HEADS, KV_HEADS, HEAD_DIM = 16, 4, 128
KV_WIDTH = KV_HEADS * HEAD_DIM
CMP_BLOCK, CMP_STRIDE = 32, 16
N_CMP = (T - CMP_BLOCK) // CMP_STRIDE + 1
N_BLOCKS = KV_HEADS * N_CMP
N_GATES = 3 * HEADS
EPS = 1e-6
NEG = -1e30
D_CONV, CONV_WIDTH = 1024, 31
D_ATTN, A_HEADS, A_DIM, CHUNK, MAX_REL = 1024, 16, 64, 64, 256
N_MEM, M_HEADS, M_DIM = 256, 4, 256
D_FF = 5632
FFN_TAPS = 3
UNIT = 256
TILE_K = 8

C_UPOOL = 0
C_GPOOL = C_UPOOL + POOL_WIDTH
C_Q = C_GPOOL + POOL_WIDTH
C_KC = C_Q + D
C_VC = C_KC + KV_WIDTH
C_KS = C_VC + KV_WIDTH
C_VS = C_KS + KV_WIDTH
C_KW = C_VS + KV_WIDTH
C_VW = C_KW + KV_WIDTH
C_GNSA = C_VW + KV_WIDTH
C_GBR = C_GNSA + D
C2_A = 0
C2_G = D_CONV
C2_Q = 2 * D_CONV
C2_K = C2_Q + D_ATTN
C2_V = C2_K + D_ATTN
C2_QM = C2_V + D_ATTN
C2_GATES = C2_QM + D_ATTN

VECS = [("norm_w", 16), ("pool_scale", 8), ("b_merge", 32), ("final_norm_w", 16), ("pe_k", 32),
        ("pe_v", 32), ("mix_norm", 16), ("mem_norm", 16), ("gate_b", 48), ("conv_w", 8 * CONV_WIDTH),
        ("conv_b", 8), ("ln_g", 8), ("ln_b", 8), ("ffn_norm", 16), ("ffn_w", 88 * FFN_TAPS),
        ("ffn_b", 88), ("final_norm_2", 16)]
VEC_AT = {}
NVEC = 0
for _name, _n in VECS:
    VEC_AT[_name] = (NVEC, _n)
    NVEC += _n

CONSTS = [("ident", P), ("ones", P), ("eps", 1), ("pad", 7), ("cos", T), ("sin", T), ("cos_c", 16), ("sin_c", 16),
          ("mask1", 512), ("mask0", 288), ("rowvalid", 2), ("rcnt", 64)]
EARLY = 2 * P + 8
CONST_AT = {}
NCONST = 0
for _name, _n in CONSTS:
    CONST_AT[_name] = (NCONST, _n)
    NCONST += _n


def shape_constants():
    c = np.zeros((P, NCONST), np.float32)

    def put(name, v):
        at, n = CONST_AT[name]
        c[:v.shape[0], at:at + v.shape[1]] = v

    half = HEAD_DIM // 2
    inv = np.float32(10000.0) ** (-np.arange(half, dtype=np.float32) / np.float32(half))
    inv = inv.astype(np.float32)

    def tables(pos):
        ang = (pos.astype(np.float32)[None, :] * inv[:, None]).astype(np.float32)
        co, si = np.cos(ang).astype(np.float32), np.sin(ang).astype(np.float32)
        return np.concatenate([co, co]), np.concatenate([-si, si])

    put("ident", np.eye(P, dtype=np.float32))
    put("ones", np.ones((P, P), np.float32))
    co, si = tables(np.arange(T))
    put("cos", co)
    put("sin", si)
    co, si = tables(np.arange(16) * CMP_STRIDE + CMP_BLOCK - 1)
    put("cos_c", co)
    put("sin_c", si)
    q = np.arange(P)[:, None]
    causal = np.where(np.arange(P)[None, :] <= q, 0.0, NEG).astype(np.float32)
    later = np.concatenate([np.zeros((P, P), np.float32), causal], 1)
    put("mask1", np.concatenate([later, later], 1))

    def cmp_mask(q0):
        n = np.arange(16)[None, :]
        ok = (n * CMP_STRIDE + CMP_BLOCK - 1 <= q0 + q) & (n < N_CMP)
        return np.where(ok, 0.0, NEG).astype(np.float32)

    put("mask0", np.concatenate([causal, causal, cmp_mask(0), cmp_mask(P)], 1))
    put("rowvalid", np.concatenate([q >= CMP_BLOCK - 1, q + P >= CMP_BLOCK - 1], 1).astype(np.float32))
    r = np.zeros((P, 4, 16), np.float32)
    for g, w in enumerate((2, 4, 8, 16)):
        r[:, g, :] = 1.0 / np.minimum(np.arange(16) + 1, w)
    put("rcnt", r.reshape(P, 64))
    put("eps", np.full((P, 1), EPS, np.float32))
    return c


class Queue:

    def __init__(self, sem):
        self.sem, self.count, self.steps, self.seen = sem, 0, [], {}

    def wait(self, *tokens):
        for sem, value in tokens:
            if value > self.seen.get(sem.name, 0):
                self.seen[sem.name] = value
                self.steps.append((sem, value))

    def run(self, fn, *tokens):
        self.wait(*tokens)
        self.count += 1
        self.steps.append(lambda e: fn(e).then_inc(self.sem, 1))
        return self.sem, self.count

    def dma(self, out, in_, sem_count, *tokens):
        self.wait(*tokens)
        sem_count[1] += 16
        sem = sem_count[0]
        self.steps.append(lambda e: e.dma_start(out, in_).then_inc(sem, 16))
        return sem, sem_count[1]

    def play(self, e):
        for s in self.steps:
            if isinstance(s, tuple):
                e.wait_ge(*s)
            else:
                s(e)


def two_blocks(nc, A, out):
    with ExitStack() as ctx:
        def sem(name):
            return ctx.enter_context(nc.semaphore(name))

        pe, act, dve, pool, sp = (Queue(sem(n)) for n in ("pe_done", "act_done", "dve_done", "pool_done", "sp_done"))

        KB = 1024
        ARENA = 207 * KB
        arena = ctx.enter_context(nc.sbuf_tensor("arena", [P, ARENA // 4], F32))
        base = nc.sbuf_base - ARENA
        names = [0]

        def at(name, kb, shape, dt=F32):
            names[0] += 1
            size = 4 * int(np.prod(shape[1:]))
            assert kb * KB + size <= ARENA, (name, kb, size)
            return nc.alloc_sbuf_tensor_at(f"{name}_{names[0]}", shape, dt, offset=base + int(kb * KB)).ap()

        RAW, HI, LO = 3, 3, 3
        raw = [at("w_raw", 8 * i, [P, TILE_K * UNIT]) for i in range(RAW)]
        w_hi = [at("w_hi", 24 + 8 * i, [P, TILE_K * UNIT], F32R) for i in range(HI)]
        w_lo = [at("w_lo", 48 + 8 * i, [P, TILE_K * UNIT], F32R) for i in range(LO)]
        RB, RA, RC, RD, RX = 72, 104, 136, 152, 168
        FREE1 = 168
        vecs = at("vecs", 195.5, [P, NVEC])
        consts = at("consts", 199.5, [P, NCONST])
        stats = at("stats", 206.25, [P, 128])

        def vec(name, i):
            a, _ = VEC_AT[name]
            return vecs[:, a + i:a + i + 1]

        def const(name, p0=0, p1=P):
            a, n = CONST_AT[name]
            return consts[p0:p1, a:a + n]

        ident, ones = const("ident"), const("ones")

        banks = [ctx.enter_context(nc.psum_tensor(f"bank{i}", [P, 512], F32)) for i in range(8)]
        main = banks[:3]
        SA, SB, TA, TB, OB = banks[3:8]

        d_x = [[sem(f"d_x{i}"), 0] for i in range(2)]
        t_const0 = act.dma(consts[:, 0:EARLY], A["consts"][:, 0:EARLY], [sem("d_const0"), 0])
        xT, memT = A["x"], A["mem"]
        chunked = lambda ap: ap.rearrange("(k p) t -> p k t", p=P)
        x_sb = at("x", RC, [P, KD, T])
        t_x = []
        for j in range(4):
            t_x += [[sp.dma(x_sb[:, 4 * j:4 * j + 4, :], chunked(xT)[:, 4 * j:4 * j + 4, :], [sem(f"d_xin{j}"), 0])]] * 2
        t_vec = sp.dma(vecs, A["vecs"], [sem("d_vec"), 0])

        d_const = [sem("d_const"), 0]
        t_const = (d_const[0], 16)

        d_raw = [[sem(f"d_raw{i}"), 0] for i in range(RAW)]
        tiles = []
        raw_free = [[] for _ in range(RAW)]
        hl_free = [None] * HI
        ready = []
        loaded = []

        def load_tile():
            i = len(loaded)
            src = tiles[i]
            nk, n = src.shape[1], src.shape[2]
            dst = raw[i % RAW][:, 0:nk * n].rearrange("p (k n) -> p k n", n=n)
            loaded.append((dst, sp.dma(dst, src, d_raw[i % RAW], *raw_free[i % RAW])))

        def split_tile(lo_on=None):
            i = len(ready)
            while len(loaded) < min(i + RAW, len(tiles)):
                load_tile()
                if len(loaded) == 2:
                    sp.dma(consts[:, EARLY:], A["consts"][:, EARLY:], d_const)
            src, t_load = loaded[i]
            nk, n = src.shape[1], src.shape[2]
            hi = w_hi[i % HI][:, 0:nk * n].rearrange("p (k n) -> p k n", n=n)
            lo = w_lo[i % LO][:, 0:nk * n].rearrange("p (k n) -> p k n", n=n)
            free = [hl_free[i % HI]] if hl_free[i % HI] else []
            t_hi = act.run(lambda e: e.activation(hi, src, ACT.Copy), t_load, *free)
            t_lo = (lo_on or dve).run(lambda e: e.tensor_tensor(lo, src, hi.bitcast(F32), ALU.subtract), t_hi, t_load, *free)
            raw_free[i % RAW] = [t_hi, t_lo]
            ready.append((hi, lo, t_hi, t_lo))
            if len(loaded) < len(tiles):
                load_tile()

        class Split:

            def __init__(self, name, kb_hi, kb_lo, nk, n=T, pad=0):
                self.flat_hi = at(name + "_hi", kb_hi, [P, nk * n + pad], F32R)
                self.flat_lo = at(name + "_lo", kb_lo, [P, nk * n + pad], F32R)
                self.hi, self.lo = (f[:, 0:nk * n].rearrange("p (k n) -> p k n", n=n) for f in (self.flat_hi, self.flat_lo))
                self.made = [None] * nk

            def make_hi(self, k0, k1, src, *tokens, lo_on=None):
                hi, lo = self.hi[:, k0:k1, :], self.lo[:, k0:k1, :]
                t_hi = act.run(lambda e: e.activation(hi, src, ACT.Copy), *tokens)

                def make_lo():
                    t_lo = (lo_on or dve).run(lambda e: e.tensor_tensor(lo, src, hi.bitcast(F32), ALU.subtract), t_hi, *tokens)
                    for k in range(k0, k1):
                        self.made[k] = (t_hi, t_lo)
                    return t_hi, t_lo
                return make_lo

            def make(self, *args):
                return self.make_hi(*args)()

        bank_free = {}

        def take(bank):
            return bank_free.get(bank.name, ())

        def give(bank, *tokens):
            bank_free[bank.name] = tokens

        def products(hi, lo, kk, moving, k, dst, cols, first):
            def fn(e):
                a = moving.hi[:, k, :]
                e.matmul(dst, hi[:, kk, cols], a, start=first, stop=True, skip_group_check=True)
                e.matmul(dst, hi[:, kk, cols], moving.lo[:, k, :], start=False, stop=True, skip_group_check=True)
                return e.matmul(dst, lo[:, kk, cols], a, start=False, stop=True, skip_group_check=True)
            return fn

        def products_token(hi, lo, kk, moving, k, dst, tok, n, first):
            def fn(e):
                a = moving.hi[:, k, tok]
                e.matmul(dst, a, hi[:, kk, 0:n], start=first, stop=True, skip_group_check=True)
                e.matmul(dst, a, lo[:, kk, 0:n], start=False, stop=True, skip_group_check=True)
                return e.matmul(dst, moving.lo[:, k, tok], hi[:, kk, 0:n], start=False, stop=True, skip_group_check=True)
            return fn

        def products_blocks(hi, lo, kk, moving, k, dst, first):
            def fn(e):
                a = slice(k * N_BLOCKS, k * N_BLOCKS + P)
                e.matmul(dst, moving.flat_hi[:, a], hi[:, kk, :], start=first, stop=True, skip_group_check=True)
                e.matmul(dst, moving.flat_hi[:, a], lo[:, kk, :], start=False, stop=True, skip_group_check=True)
                return e.matmul(dst, moving.flat_lo[:, a], hi[:, kk, :], start=False, stop=True, skip_group_check=True)
            return fn

        def products_narrow(slot, kk, moving, k, dst, first):
            def fn(e):
                a = slice(kk * N_GATES, kk * N_GATES + P)
                hi, lo, x = w_hi[slot % HI], w_lo[slot % LO], moving.hi[:, k, :]
                e.matmul(dst, hi[:, a], x, start=first, stop=True, skip_group_check=True)
                e.matmul(dst, hi[:, a], moving.lo[:, k, :], start=False, stop=True, skip_group_check=True)
                return e.matmul(dst, lo[:, a], x, start=False, stop=True, skip_group_check=True)
            return fn

        jobs = []
        side = []
        LOOK = 2

        def unit(w, rows, col, moving, evac, kind="channel", n=UNIT, before=None, after=None, k0=0):
            nk = (rows[1] - rows[0]) // P
            if kind == "narrow":
                view = w.rearrange("p (k n) -> p k n", n=n)
            else:
                view = w[rows[0]:rows[1], col:col + n].rearrange("(k p) n -> p k n", p=P)
            step = TILE_K if n == UNIT else nk
            parts = [(k, min(k + step, nk)) for k in range(0, nk, step)]
            for a, b in parts:
                tiles.append(view[:, a:b, :])
            jobs.append(dict(parts=parts, n=n, moving=moving, evac=evac, kind=kind, before=before, after=after, k0=k0))

        def advance():
            for g in list(side):
                try:
                    next(g)
                except StopIteration:
                    side.remove(g)

        def later(n, g):
            for _ in range(n):
                yield
            return (yield from g)

        def finish(*gens):
            while any(g in side for g in gens):
                advance()

        def spawn(g):
            side.append(g)
            return g

        def drive():
            at_tile = 0
            for j, job in enumerate(jobs):
                if job["before"]:
                    job["before"]()
                bank = main[j % 3]
                n = job["n"]
                tok = None
                for a, b in job["parts"]:
                    while len(ready) < min(at_tile + 1 + LOOK, len(tiles)):
                        split_tile()
                    hi, lo, t_hi, t_lo = ready[at_tile]
                    pe.wait(t_hi, t_lo, *(take(bank) if a == 0 else ()))
                    mv = job["moving"]
                    outer = range(1) if job["kind"] in ("blocks", "narrow") else range(2)
                    for o in outer:
                        for kk in range(b - a):
                            k = job["k0"] + a + kk
                            first = a == 0 and o == 0 and kk == 0
                            pe.wait(*mv.made[k])
                            if job["kind"] == "channel":
                                f = products(hi, lo, kk, mv, k, bank[:, o * T:(o + 1) * T], slice(o * P, (o + 1) * P), first)
                            elif job["kind"] == "blocks":
                                pe.wait(*mv.made[min(k + 2, CMP_BLOCK - 1)])
                                f = products_blocks(hi, lo, kk, mv, k, bank[:, 0:T], first)
                            elif job["kind"] == "narrow":
                                f = products_narrow(at_tile, kk, mv, k, bank[:, 0:T], first)
                            else:
                                f = products_token(hi, lo, kk, mv, k, bank[:, o * T:o * T + n], slice(o * P, (o + 1) * P), n, first)
                            if o == outer[-1] and kk == b - a - 1:
                                tok = pe.run(f)
                            else:
                                pe.steps.append(f)
                    hl_free[at_tile % HI] = tok
                    at_tile += 1
                    if b < job["parts"][-1][1]:
                        advance()
                give(bank, *job["evac"](bank, tok))
                if job["after"]:
                    job["after"](tok)
                advance()
            while side:
                advance()

        sumsq = at("sumsq", 188, [P, T])
        rstd = at("rstd", 189, [P, T])
        sq = [at("sq", 184 + 2 * i, [P, 2, T]) for i in range(2)]
        sq_read = [(), ()]

        def last(q):
            return q.sem, q.count

        def column_sum(src, bank, *tokens):
            return pe.run(lambda e: e.matmul(bank[:, 0:T], ones, src, start=True, stop=True), t_const0, *tokens, *take(bank))

        def inverse_std(t_sum, bank, n):
            eps = const("eps")
            t = act.run(lambda e: e.activation(rstd, bank[:, 0:T], ACT.Sqrt, bias=eps, scale=1.0 / n), t_sum, t_const0, last(dve))
            give(bank, t)
            return dve.run(lambda e: e.reciprocal(rstd, rstd), t)

        def mean_square(src, tokens):
            for j in range(KD // 2):
                while len(tokens) <= j:
                    yield
                s, v = sq[j % 2], src[:, 2 * j:2 * j + 2, :]
                t_sq = act.run(lambda e, s=s, v=v: e.activation(s, v, ACT.Square), *tokens[j], *sq_read[j % 2])
                a, b = s[:, 0, :], s[:, 1, :]
                if j == 0:
                    t = dve.run(lambda e, a=a, b=b: e.tensor_tensor(sumsq, a, b, ALU.add), t_sq, last(pe))
                else:
                    t = dve.run(lambda e, a=a: e.tensor_tensor(sumsq, sumsq, a, ALU.add), t_sq, t)
                    t = dve.run(lambda e, b=b: e.tensor_tensor(sumsq, sumsq, b, ALU.add), t)
                sq_read[j % 2] = (t,)
                if j % 2:
                    yield
            yield
            t_sum = column_sum(sumsq, TB, t)
            yield
            return inverse_std(t_sum, TB, D)

        def mean_square_first(src, tokens, squares):
            for j in range(KD // 2):
                s, v = squares[:, 2 * j:2 * j + 2, :], src[:, 2 * j:2 * j + 2, :]
                if j % 2 == 0:
                    t = act.run(lambda e, s=s, v=v: e.activation(s, v, ACT.Square), *tokens[j])
                else:
                    t = dve.run(lambda e, s=s, v=v: e.tensor_tensor(s, v, v, ALU.mult), *tokens[j])
                a, b = s[:, 0, :], s[:, 1, :]
                t = dve.run(lambda e, a=a, b=b: e.tensor_tensor(a, a, b, ALU.add), t)
                t_sum = pe.run(lambda e, j=j, a=a: e.matmul(TB[:, 0:T], ones, a, start=j == 0, stop=j == KD // 2 - 1),
                               t_const0, t)
            yield
            return inverse_std(t_sum, TB, D)

        def rms_norm(src, tokens, gain, dst, split, *split_free, first_squares=None, lo_on=None, done=None):
            if first_squares is not None:
                t_rstd = yield from mean_square_first(src, tokens, first_squares)
            else:
                t_rstd = yield from mean_square(src, tokens)
            yield
            done, pending = [] if done is None else done, None
            for j in range(KD // 2):
                d = dst[:, 2 * j:2 * j + 2, :] if dst is not None else sq[j % 2]
                free = sq_read[j % 2] if dst is None else ()
                for c in range(2):
                    t = dve.run(lambda e, d=d, c=c, k=2 * j + c: e.scalar_tensor_tensor(
                        d[:, c, :], src[:, k, :], vec(gain, k), rstd, ALU.mult, ALU.mult), t_rstd, t_vec, *tokens[j], *free)
                if split is not None:
                    make_lo = split.make_hi(2 * j, 2 * j + 2, d, t, *split_free, lo_on=lo_on)
                    if pending:
                        pending()

                    def pending(make_lo=make_lo, j=j):
                        t_hl = make_lo()
                        if dst is None:
                            sq_read[j % 2] = t_hl
                done.append((t,))
                if j % 2:
                    yield
            if pending:
                pending()
            return done

        def preload_sqrt():
            act.run(lambda e: e.activation(stats[:, 120:121], const("eps"), ACT.Sqrt), t_const0)

        h = Split("h", RA, RA + 16, KD)

        q1 = at("q", RB, [P, HEADS, T])
        k_sel = at("k_sel", RB + 16, [P, KV_HEADS, T])
        k_win = at("k_win", RB + 20, [P, KV_HEADS, T])
        v_sel = at("v_sel", RB + 24, [P, 2, KV_WIDTH])
        v_win = at("v_win", RB + 28, [P, 2, KV_WIDTH])
        raw_c = [at("kc_raw", RC, [P, KV_HEADS, T]), at("vc_raw", RC + 4, [P, KV_HEADS, T])]
        kb = at("kb", RC + 8, [P, CMP_BLOCK, KV_HEADS * N_CMP])
        kb_split = Split("kb", RD, RD + 8, CMP_BLOCK, N_BLOCKS, pad=P - N_BLOCKS)
        pad_from = CMP_BLOCK * N_BLOCKS
        evac_tmp = [at("evac_tmp", FREE1 + 2 * i, [P, 2, T]) for i in range(2)]
        s_buf = [at("scores", FREE1 + 4 + 3.125 * i, [P, 800]) for i in range(2)]
        pt_buf = at("pT", FREE1 + 10.25, [P, 1024])
        kc_t = at("kc", FREE1 + 14.25, [P, KV_HEADS, 16])
        gate6 = at("gate6", FREE1 + 14.5, [P, HEADS, 6])
        hid = at("hid", FREE1 + 14.875, [P, 2, KV_HEADS * N_CMP])
        vc_t = at("vc", FREE1 + 15.375, [16, KV_HEADS, HEAD_DIM])
        tmp_free = [(), ()]

        t_half = []

        def halve_biases():
            for name in ("b_merge", "gate_b"):
                a, n = VEC_AT[name]
                v = vecs[:, a:a + n]
                t_half.append(dve.run(lambda e, v=v: e.tensor_scalar(v, v, 0.5, None, ALU.mult), t_vec))

        rope_turn = [0]

        def rope_to(dst, note):
            def evac(bank, tok):
                i = rope_turn[0] % 2
                rope_turn[0] += 1
                sw = evac_tmp[i]
                z = bank[:, :].rearrange("p (c t) -> p c t", c=2)
                cos = const("cos").unsqueeze(1).broadcast_to([P, 2, T])
                sin = const("sin").unsqueeze(1).broadcast_to([P, 2, T])
                act.run(lambda e: e.copy(sw[0:64, :, :], z[64:128, :, :]), tok, *tmp_free[i])
                t_sw = act.run(lambda e: e.copy(sw[64:128, :, :], z[0:64, :, :]))
                t0 = dve.run(lambda e: e.tensor_tensor(dst, z, cos, ALU.mult), tok, t_sw, t_const)
                t1 = dve.run(lambda e: e.tensor_tensor(sw, sw, sin, ALU.mult), t_sw)
                t2 = dve.run(lambda e: e.tensor_tensor(dst, dst, sw, ALU.add), t0, t1)
                tmp_free[i] = (t2,)
                note.append(t2)
                return t_sw, t0
            return evac

        def to_sbuf(dst, scale=1.0, note=None):
            def evac(bank, tok):
                src = bank[:, :].rearrange("p (c t) -> p c t", c=2)
                t = act.run(lambda e: e.activation(dst, src, ACT.Copy, scale=scale), tok)
                if note is not None:
                    note.append(t)
                return (t,)
            return evac

        preload_sqrt()
        x_squares = at("x_squares", RA, [P, KD, T])
        g_h = spawn(rms_norm(x_sb, t_x, "norm_w", None, h, first_squares=x_squares))

        def first_norm():
            for _ in range(2):
                advance()
            for _ in range(3):
                split_tile(lo_on=pool)
                advance()
            finish(g_h)
            halve_biases()

        w_in = A["w_in"]
        rows = (0, D)

        n_raw = [[], []]
        for s, col in enumerate((C_KC, C_VC)):
            for u in range(2):
                unit(w_in, rows, col + u * UNIT, h, to_sbuf(raw_c[s][:, 2 * u:2 * u + 2, :], note=n_raw[s]),
                     before=first_norm if s == 0 and u == 0 else None,
                 after=(lambda tok: start_blocks(0)) if s == 0 and u == 1 else None)
        n_k = []

        kb_free = [()]
        cmp_out = {}

        def blocks(s):
            name = ("pe_k", "pe_v")[s]
            kb4 = kb.rearrange("p l (h n) -> p l h n", h=KV_HEADS)
            t_kb = []
            for l in range(CMP_BLOCK):
                src = raw_c[s][:, :, l:l + CMP_STRIDE * (N_CMP - 1) + 1:CMP_STRIDE]
                t = pool.run(lambda e, l=l, src=src: e.tensor_scalar(kb4[:, l, :, :], src, vec(name, l), None, ALU.add),
                             *n_raw[s], t_vec, *kb_free[0])
                if l % 8 == 7:
                    t_kb.append(t)
            yield
            while s == 1 and "cmp0" not in cmp_out:
                yield
            for i in range(4):
                yield
                kb_free[0] = kb_split.make(8 * i, 8 * i + 8, kb[:, 8 * i:8 * i + 8, :], t_kb[i],
                                           *([cmp_out["cmp0"]] if s else []))
                yield

        pool.run(lambda e: e.memset(kb_split.flat_hi[:, pad_from:].bitcast(F32), 0.0))
        t_pad = pool.run(lambda e: e.memset(kb_split.flat_lo[:, pad_from:].bitcast(F32), 0.0))

        g_blocks = [None, None]

        def cmp_evac(s):
            def evac(bank, tok):
                z = bank[0:N_BLOCKS, 0:T]
                th = evac_tmp[0][0:N_BLOCKS, 0, :]
                t = act.run(lambda e: e.activation(th, z, ACT.Tanh, scale=0.5), tok, *tmp_free[0])
                t = dve.run(lambda e: e.scalar_tensor_tensor(hid_rows, th, 1.0, z, ALU.add, ALU.mult), t,
                            *((cmp_out["rows_read"],) if s else ()))
                tmp_free[0] = (t,)
                cmp_out["rows%d" % s] = t
                cmp_out["cmp%d" % s] = tok
                spawn(second_layer(s))
                return (t,)
            return evac

        w2_sb = [at("w2k", 190, [P, 2, HEAD_DIM]), at("w2v", 191, [P, 2, HEAD_DIM])]
        t_w2 = [act.dma(w2_sb[s], A["cmp_w2_" + "kv"[s]].rearrange("(k p) n -> p k n", p=P), [sem("d_w2" + "kv"[s]), 0])
                for s in range(2)]
        gate_rows = at("gate_rows", 193.5, [N_GATES, T])
        hid_rows = at("hid_rows", 192.5, [N_BLOCKS, T])
        kc_raw2 = at("kc2", 192, [P, KV_HEADS, N_CMP])
        kc_sw = at("kcsw", 192.25, [P, KV_HEADS, N_CMP])

        def second_layer(s):
            yield

            def turn(e):
                for f in range(2):
                    m = e.transpose(TA[:, f * 64:f * 64 + N_BLOCKS], hid_rows[:, f * P:(f + 1) * P],
                                    ident[0:N_BLOCKS, 0:N_BLOCKS])
                return m
            t = pe.run(turn, cmp_out["rows%d" % s], t_const, *take(TA))
            cmp_out["rows_read"] = t
            v = TA[:, 0:128].rearrange("p (f n) -> p f n", f=2)[:, :, 0:N_BLOCKS]
            t = act.run(lambda e: e.copy(hid, v), t, *((cmp_out["hid_read"],) if s else ()))
            give(TA, t)
            cmp_out["hid%d" % s] = t
            yield
            if s == 0:
                ps = TA[:, 0:KV_HEADS * N_CMP]

                def mm(e):
                    for f in range(2):
                        m = e.matmul(ps, w2_sb[0][:, f, :], hid[:, f, :], start=f == 0, stop=f == 1)
                    return m
                t = pe.run(mm, cmp_out["hid0"], t_w2[0], *take(TA))
                cmp_out["hid_read"] = t
                z = ps.rearrange("p (h n) -> p h n", h=KV_HEADS)
                shape = [P, KV_HEADS, N_CMP]
                cos = const("cos_c")[:, 0:N_CMP].unsqueeze(1).broadcast_to(shape)
                sin = const("sin_c")[:, 0:N_CMP].unsqueeze(1).broadcast_to(shape)
                yield
                t_z = dve.run(lambda e: e.memset(kc_t, 0.0))
                act.run(lambda e: e.activation(kc_sw[0:64], z[64:128], ACT.Copy, scale=0.5), t)
                t_sw = act.run(lambda e: e.activation(kc_sw[64:128], z[0:64], ACT.Copy, scale=0.5))
                t0 = dve.run(lambda e: e.scalar_tensor_tensor(kc_raw2, z, 0.5, cos, ALU.mult, ALU.mult), t, t_sw, t_const)
                t1 = dve.run(lambda e: e.tensor_tensor(kc_sw, kc_sw, sin, ALU.mult), t_sw)
                t2 = dve.run(lambda e: e.tensor_tensor(kc_t[:, :, 0:N_CMP], kc_raw2, kc_sw, ALU.add), t0, t1, t_z)
                give(TA, t_sw, t0)
                cmp_out["kc"] = t2
            else:
                def mm(e):
                    for hh in range(KV_HEADS):
                        for f in range(2):
                            m = e.matmul(TA[0:N_CMP, hh * P:(hh + 1) * P], hid[:, f, hh * N_CMP:(hh + 1) * N_CMP],
                                         w2_sb[1][:, f, :], start=f == 0, stop=f == 1)
                    return m
                t = pe.run(mm, cmp_out["hid1"], t_w2[1], *take(TA))
                yield
                t = act.run(lambda e: e.activation(vc_t[0:N_CMP], TA[0:N_CMP, :].rearrange("p (h n) -> p h n", h=KV_HEADS),
                                                   ACT.Copy, scale=0.5), t)
                give(TA, t)
                cmp_out["vc"] = t

        def start_blocks(s):
            g_blocks[s] = spawn(blocks(s))

        for u in range(2):
            unit(w_in, rows, C_KS + u * UNIT, h, rope_to(k_sel[:, 2 * u:2 * u + 2, :], n_k))
        for u in range(2):
            unit(w_in, rows, C_KW + u * UNIT, h, rope_to(k_win[:, 2 * u:2 * u + 2, :], n_k))

        def cmp_unit(s):
            w = A["cmp_w1_" + "kv"[s]].rearrange("l d f -> (l d) f")
            unit(w, (0, CMP_BLOCK * HEAD_DIM), 0, kb_split, cmp_evac(s), kind="blocks", before=lambda: (finish(g_blocks[s]), pe.wait(t_pad)))

        cmp_unit(0)
        jobs[-1]["after"] = lambda tok: start_blocks(1)
        for u in range(2):
            unit(w_in, rows, C_VS + u * UNIT, h, to_sbuf(v_sel[:, :, u * UNIT:(u + 1) * UNIT], note=n_k), kind="token")
        for u in range(2):
            unit(w_in, rows, C_VW + u * UNIT, h, to_sbuf(v_win[:, :, u * UNIT:(u + 1) * UNIT], note=n_k), kind="token")
        def gates_evac(bank, tok):
            th = gate_rows
            t_z = act.run(lambda e: e.activation(th, bank[0:N_GATES, 0:T], ACT.Tanh, scale=0.5), tok)
            t = dve.run(lambda e: e.tensor_scalar(th, th, 0.5, 0.5, ALU.mult, ALU.add), t_z)

            def turn(e):
                for qt in range(2):
                    m = e.transpose(TB[:, qt * 64:qt * 64 + N_GATES], th[:, qt * P:(qt + 1) * P], ident[0:N_GATES, 0:N_GATES])
                return m

            def place():
                yield
                t_t = pe.run(turn, t, t_const, *take(TB))
                yield
                g = lambda qt, br: TB[:, qt * 64:qt * 64 + N_GATES].rearrange("p (h b) -> p h b", b=3)[:, :, br]
                for i, (qt, br) in enumerate(((1, 1), (1, 2), (0, 1), (0, 2))):
                    dve.run(lambda e, i=i, v=g(qt, br): e.tensor_copy(gate6[:, :, i], v), t_t)
                rv = const("rowvalid")
                for i in range(2):
                    t_g = dve.run(lambda e, i=i, v=g(i, 0): e.tensor_scalar(gate6[:, :, 4 + i], v, rv[:, i:i + 1], None, ALU.mult))
                give(TB, t_g)
                cmp_out["gates"] = t_g

            spawn(place())
            return (t_z,)

        unit(A["w_gates"], rows, 0, h, gates_evac, kind="narrow", n=N_GATES)
        n_q = []
        for u in range(8):
            if u == 1:
                cmp_unit(1)
            unit(w_in, rows, C_Q + u * UNIT, h, rope_to(q1[:, 2 * u:2 * u + 2, :], n_q),
                 after=(lambda tok: spawn(attention1())) if u == 7 else None)

        SC1 = HEAD_DIM ** -0.5
        HEAD_SLOTS = 4
        s_free, head_done = [(), ()], [None] * HEADS
        pt_free = [()]

        def head1(hd):
            kv, b = hd // (HEADS // KV_HEADS), hd % 2
            S = s_buf[b]
            st = stats[:, 16 * b:16 * b + 16]
            mx, sm = st[:, 0:6], st[:, 6:12]
            q0_, q1_ = q1[:, hd, 0:P], q1[:, hd, P:T]

            def score(e):
                e.matmul(SA[:, 0:T], q1_, k_sel[:, kv, :], start=True, stop=True)
                e.matmul(SA[:, T:2 * T], q1_, k_win[:, kv, :], start=True, stop=True)
                e.matmul(SB[:, 0:P], q0_, k_sel[:, kv, 0:P], start=True, stop=True)
                e.matmul(SB[:, P:2 * P], q0_, k_win[:, kv, 0:P], start=True, stop=True)
                e.matmul(SB[:, 256:272], q0_, kc_t[:, kv, :], start=True, stop=True)
                return e.matmul(SB[:, 272:288], q1_, kc_t[:, kv, :], start=True, stop=True)
            t_s = pe.run(score, n_q[hd // 2], *n_k, cmp_out["kc"], *take(SA), *take(SB))
            yield
            t_a = dve.run(lambda e: e.scalar_tensor_tensor(S[:, 0:512], SA[:, :], SC1, const("mask1"), ALU.mult, ALU.add),
                          t_s, *s_free[b])
            t_b = dve.run(lambda e: e.scalar_tensor_tensor(S[:, 512:800], SB[:, 0:288], SC1, const("mask0"), ALU.mult, ALU.add))
            give(SA, t_a)
            give(SB, t_b)
            segs = [(0, 256), (256, 256), (512, 128), (640, 128), (768, 16), (784, 16)]
            groups = [(0, 2, 256), (2, 2, 128), (4, 2, 16)]
            for i, m, n in groups:
                v = S[:, segs[i][0]:segs[i][0] + m * n].rearrange("p (m n) -> p m n", m=m)
                t_m = dve.run(lambda e, v=v, i=i, m=m: e.tensor_reduce(mx[:, i:i + m], v, AX.X, ALU.max), t_a, t_b)
            t_m = dve.run(lambda e: e.tensor_scalar(mx, mx, -1.0, None, ALU.mult), t_m)
            yield
            for i, (o, n) in enumerate(segs):
                v = S[:, o:o + n]
                t_e = act.run(lambda e, v=v, i=i: e.activation(v, v, ACT.Exp, bias=mx[:, i:i + 1], accum_out=sm[:, i:i + 1]), t_m)
            yield
            t = dve.run(lambda e: e.reciprocal(sm, sm), t_e)
            t = dve.run(lambda e: e.tensor_tensor(sm, sm, gate6[:, hd, :], ALU.mult), t, cmp_out["gates"])
            for i, m, n in groups:
                v = S[:, segs[i][0]:segs[i][0] + m * n].rearrange("p (m n) -> p m n", m=m)
                c = sm[:, i:i + m].unsqueeze(2).broadcast_to([P, m, n])
                t_p = pool.run(lambda e, v=v, c=c: e.tensor_tensor(v, v, c, ALU.mult), t)
            yield
            yield

            def flip(e):
                e.transpose(TA[:, 0:P], S[:, 512:640], ident)
                e.transpose(TA[:, P:2 * P], S[:, 0:P], ident)
                e.transpose(TA[:, 2 * P:3 * P], S[:, 640:768], ident)
                e.transpose(TA[:, 3 * P:4 * P], S[:, 256:384], ident)
                e.transpose(TB[:, 0:P], S[:, P:2 * P], ident)
                e.transpose(TB[:, P:2 * P], S[:, 384:512], ident)
                e.transpose(TB[0:16, 2 * P:3 * P], S[:, 768:784], ident)
                return e.transpose(TB[0:16, 3 * P:4 * P], S[:, 784:800], ident)
            t_t = pe.run(flip, t_p, *take(TA), *take(TB))
            s_free[b] = (t_t,)
            yield
            pt = pt_buf
            t0 = act.run(lambda e: e.copy(pt[:, 0:512], TA[:, :]), t_t, *pt_free[0])
            t1 = dve.run(lambda e: e.tensor_copy(pt[:, 512:768], TB[:, 0:256]), t_t, *pt_free[0])
            t2 = dve.run(lambda e: e.tensor_copy(pt[0:16, 768:1024], TB[0:16, 256:512]))
            give(TA, t0)
            give(TB, t1, t2)
            yield
            yield

            def values(e):
                c = slice(kv * P, (kv + 1) * P)
                e.matmul(OB[:, 0:T], v_sel[:, 0, c], pt[:, 0:256], start=True, stop=False, skip_group_check=True)
                e.matmul(OB[:, 0:T], v_win[:, 0, c], pt[:, 256:512], start=False, stop=False, skip_group_check=True)
                e.matmul(OB[:, 0:T], vc_t[0:N_CMP, kv, :], pt[0:N_CMP, 768:1024], start=False, stop=False, skip_group_check=True)
                e.matmul(OB[:, P:T], v_sel[:, 1, c], pt[:, 512:640], start=False, stop=False, skip_group_check=True)
                return e.matmul(OB[:, P:T], v_win[:, 1, c], pt[:, 640:768], start=False, stop=True, skip_group_check=True)
            t_v = pe.run(values, t0, t1, t2, *n_k, cmp_out["vc"], *take(OB))
            pt_free[0] = (t_v,)
            yield
            t_o = act.run(lambda e: e.copy(q1[:, hd, :], OB[:, 0:T]), t_v)
            give(OB, t_o)
            head_done[hd] = t_o

        def attention1():
            for hd in range(HEADS):
                g = spawn(head1(hd))
                next(g)
                for _ in range(HEAD_SLOTS):
                    yield

        pgate = at("pool_gate", RC, [P, 8, T])
        pu = at("pool_u", FREE1 + 17.375, [P, 2, T])
        pp = [at("pool_sum", FREE1 + 19.375 + 2 * i, [P, 2, T]) for i in range(2)]
        pooled = Split("pooled", FREE1 + 23.375, FREE1 + 25.375, 2)
        ypool = Split("ypool", RD, RD + 8, 8)
        pool_free = {"pu": (), "pp": (), "split": ()}
        n_pg = []

        def gpool_evac(j):
            def evac(bank, tok):
                th = evac_tmp[j % 2]
                z = bank[:, :].rearrange("p (c t) -> p c t", c=2)
                t = act.run(lambda e: e.activation(th, z, ACT.Tanh, scale=0.5), tok, *tmp_free[j % 2])
                t = dve.run(lambda e: e.scalar_tensor_tensor(pgate[:, 2 * j:2 * j + 2, :], th, 1.0, z, ALU.add, ALU.mult),
                            t, *kb_free[0], last(pool))
                tmp_free[j % 2] = (t,)
                n_pg.append(t)
                return (t,)
            return evac

        def upool_evac(g):
            def evac(bank, tok):
                w = 2 << g
                z = bank[:, :].rearrange("p (c t) -> p c t", c=2)
                t_u = act.run(lambda e: e.copy(pu, z), tok, *pool_free["pu"], cmp_out["vc"])
                src, t_prev = pu, t_u
                free = pool_free["pp"]
                for i in range(g + 1):
                    d = 1 << i
                    dst = pp[i % 2]
                    t0 = dve.run(lambda e, s=src, o=dst, d=d: e.tensor_tensor(o[:, :, d:], s[:, :, d:], s[:, :, :T - d], ALU.add),
                                 t_prev, *free)
                    t_prev = dve.run(lambda e, s=src, o=dst, d=d: e.tensor_copy(o[:, :, 0:d], s[:, :, 0:d]), t_prev, t0)
                    src = dst
                rc = const("rcnt")[:, 16 * g:16 * g + 16].unsqueeze(1).broadcast_to([P, 2, 16])
                ta = dve.run(lambda e, s=src: e.tensor_tensor(s[:, :, 0:16], s[:, :, 0:16], rc, ALU.mult), t_prev, t_const)
                tb = dve.run(lambda e, s=src: e.scalar_tensor_tensor(pu[:, :, 16:], s[:, :, 16:], 1.0 / w, pu[:, :, 16:],
                                                                     ALU.mult, ALU.subtract), t_prev)
                tc = dve.run(lambda e, s=src: e.tensor_tensor(pu[:, :, 0:16], s[:, :, 0:16], pu[:, :, 0:16], ALU.subtract), ta)
                t_hl = pooled.make(0, 2, pu, tb, tc, *pool_free["split"])
                pool_free["pu"] = t_hl
                pool_free["pp"] = (tc,)
                return (t_u,)
            return evac

        def mix_evac(g):
            def evac(bank, tok):
                pool_free["split"] = (tok,)
                y = pp[0]
                for c in range(2):
                    k = 2 * g + c
                    t = dve.run(lambda e, c=c, k=k: e.scalar_tensor_tensor(
                        y[:, c, :], bank[:, c * T:(c + 1) * T], vec("pool_scale", k), pgate[:, k, :], ALU.mult, ALU.mult),
                        tok, n_pg[g], *pool_free["pp"])
                t_hl = ypool.make(2 * g, 2 * g + 2, y, t, *kb_free[0], cmp_out["kb_read"])
                pool_free["pp"] = t_hl
                return (t,)
            return evac

        for j in range(4):
            unit(w_in, rows, C_GPOOL + j * UNIT, h, gpool_evac(j))
            if j >= 1:
                unit(A["pool_mix"][j - 1], (0, UNIT), 0, pooled, mix_evac(j - 1))
            unit(w_in, rows, C_UPOOL + j * UNIT, h, upool_evac(j),
                 before=(lambda: cmp_out.__setitem__("kb_read", last(pe))) if j == 0 else None)

        ma = at("merged_a", RC, [P, KD, T])
        gm1 = at("gate_b1", RD, [P, KD, T])
        gate_t = {}
        n_ma, n_gm1 = [], []

        def gate0_evac(c):
            def evac(bank, tok):
                th = evac_tmp[c % 2]
                for i in range(2):
                    t = act.run(lambda e, i=i: e.activation(th[:, i, :], bank[:, i * T:(i + 1) * T], ACT.Tanh,
                                                            bias=vec("b_merge", 2 * c + i), scale=0.5), tok, *t_half, *tmp_free[c % 2])
                gate_t[c] = t
                return (t,)
            return evac

        def ya_evac(c):
            def evac(bank, tok):
                th = evac_tmp[c % 2]
                z = bank[:, :].rearrange("p (c t) -> p c t", c=2)
                t = dve.run(lambda e: e.scalar_tensor_tensor(ma[:, 2 * c:2 * c + 2, :], th, 1.0, z, ALU.add, ALU.mult),
                            tok, gate_t[c], *ypool.made[7])
                tmp_free[c % 2] = (t,)
                n_ma.append(t)
                return (t,)
            return evac

        def ya_unit(c):
            unit(A["w_pool_out"], (0, POOL_WIDTH), c * UNIT, ypool, ya_evac(c),
                 after=(lambda tok: gate_t.__setitem__("ypool_read", tok)) if c == 7 else None)

        for c in range(8):
            unit(A["w_merge"], rows, c * UNIT, h, gate0_evac(c))
            if c == 0:
                unit(A["pool_mix"][3], (0, UNIT), 0, pooled, mix_evac(3))
            else:
                ya_unit(c - 1)
        ya_unit(7)

        def gate1_evac(c):
            def evac(bank, tok):
                for i in range(2):
                    t = act.run(lambda e, i=i: e.activation(gm1[:, 2 * c + i, :], bank[:, i * T:(i + 1) * T], ACT.Tanh,
                                                            bias=vec("b_merge", 16 + 2 * c + i), scale=0.5),
                                tok, *t_half, gate_t["ypool_read"])
                n_gm1.append(t)
                return (t,)
            return evac

        for c in range(8):
            unit(A["w_merge"], rows, D + c * UNIT, h, gate1_evac(c))

        n_o = []

        def gnsa_evac(c):
            def evac(bank, tok):
                th = evac_tmp[c % 2]
                z = bank[:, :].rearrange("p (c t) -> p c t", c=2)
                o = q1[:, 2 * c:2 * c + 2, :]
                t = act.run(lambda e: e.activation(th, z, ACT.Tanh, scale=0.5), tok, *tmp_free[c % 2])
                t_z = dve.run(lambda e: e.scalar_tensor_tensor(th, th, 1.0, z, ALU.add, ALU.mult), t)
                t = dve.run(lambda e: e.tensor_tensor(o, o, th, ALU.mult), t_z, head_done[2 * c], head_done[2 * c + 1])
                tmp_free[c % 2] = (t,)
                n_o.append(t)
                return (t_z,)
            return evac

        def wait_heads(c):
            def f():
                while head_done[2 * c + 1] is None:
                    advance()
            return f

        o_split = Split("o", RA, RA + 16, KD)

        def split_o(tok):
            for c in range(8):
                o_split.make(2 * c, 2 * c + 2, q1[:, 2 * c:2 * c + 2, :], n_o[c], tok)

        for c in range(8):
            unit(w_in, rows, C_GNSA + c * UNIT, h, gnsa_evac(c), before=wait_heads(c),
                 after=split_o if c == 7 else None)

        merged = Split("merged", RB, RB + 16, KD)
        xr = [at("x_again", FREE1 + 8 + 2 * i, [P, 2, T]) for i in range(2)]
        mtmp = [at("merge_tmp", FREE1 + 4 + 2 * i, [P, 2, T]) for i in range(2)]
        mtmp_free = [(), ()]

        def yb_evac(c):
            def evac(bank, tok):
                m = mtmp[c % 2]
                z = bank[:, :].rearrange("p (c t) -> p c t", c=2)
                t_z = dve.run(lambda e: e.scalar_tensor_tensor(m, gm1[:, 2 * c:2 * c + 2, :], 1.0, z, ALU.add, ALU.mult),
                              tok, n_gm1[c], *mtmp_free[c % 2], *s_free[0], *s_free[1])
                t = dve.run(lambda e: e.tensor_tensor(m, m, ma[:, 2 * c:2 * c + 2, :], ALU.add), t_z, n_ma[c])
                mtmp_free[c % 2] = merged.make(2 * c, 2 * c + 2, m, t, *o_split.made[15], *pt_free[0], head_done[15])
                return (t_z,)
            return evac

        for c in range(8):
            unit(A["w_nsa_out"], rows, c * UNIT, o_split, yb_evac(c))

        mem_sb = at("mem", RC, [P, KD, T])
        mn = Split("mn", RA, RA + 16, KD)
        d_mem = [[sem(f"d_mem{j}"), 0] for j in range(4)]
        g_mem = [None]

        def start_mem(tok):
            read = (last(dve), tok)
            t = [act.dma(mem_sb[:, 4 * j:4 * j + 4, :], chunked(memT)[:, 4 * j:4 * j + 4, :], d_mem[j], *read) for j in range(4)]
            g_norms[0] = spawn(norms_between())
            g_mem[0] = spawn(later(2, rms_norm(mem_sb, [[t[j // 2]] for j in range(8)], "mem_norm", None, mn, tok, lo_on=pool)))
        jobs[-1]["after"] = start_mem

        x1 = at("x1", RD, [P, KD, T])
        t_xr = {}
        n_x1, x1_tokens = [], []

        def load_x(c):
            def f():
                t_xr[c] = act.dma(xr[c % 2], chunked(xT)[:, 2 * c:2 * c + 2, :], d_x[c % 2],
                                  *([n_x1[c - 2]] if c >= 2 else [last(pe)]))
            return f

        def wout_evac(c):
            def evac(bank, tok):
                z = bank[:, :].rearrange("p (c t) -> p c t", c=2)
                t = dve.run(lambda e: e.scalar_tensor_tensor(x1[:, 2 * c:2 * c + 2, :], z, 0.25, xr[c % 2], ALU.mult, ALU.add),
                            tok, t_xr[c], *merged.made[15])
                n_x1.append(t)
                x1_tokens.append((t,))
                return (t,)
            return evac

        for c in range(8):
            unit(A["w_out"], rows, c * UNIT, merged, wout_evac(c), before=load_x(c))

        x2_dram = nc.dram_tensor("x2_scratch", (P, KD * T), F32).ap().rearrange("p (k t) -> p k t", k=KD)
        xn = Split("xn", RB, RB + 16, KD)
        k_mem = at("k_mem", RC, [P, 8, T])
        v_mem = at("v_mem", RC + 8, [P, 2, D_ATTN])
        n_km = []
        d_x2 = [sem("d_x2"), 0]

        def norms_between():
            while g_mem[0] in side:
                yield
            done = []

            def final_norm():
                yield from rms_norm(x1, x1_tokens, "final_norm_w", x1, None, done=done)
                b2["x2"] = [act.dma(x2_dram, x1, d_x2, done[-1][0])]
            spawn(final_norm())
            while not done:
                yield
            yield from rms_norm(x1, done, "mix_norm", None, xn, b2["wout"])
            b2["xn"] = xn.made[15]
            e2_free[:] = sq_read

        b2 = {}
        g_norms = [None]

        e2_free = [(), ()]

        def after_wout(tok):
            b2["wout"] = tok

        jobs[-1]["after"] = after_wout
        for u in range(4):
            unit(A["w_mem_kv"], rows, u * UNIT, mn,
                 to_sbuf(k_mem[:, 2 * u:2 * u + 2, :], note=n_km), before=(lambda: finish(g_mem[0])) if u == 0 else None)
        for u in range(4):
            unit(A["w_mem_kv"], rows, D_ATTN + u * UNIT, mn,
                 to_sbuf(v_mem[:, :, u * UNIT:(u + 1) * UNIT], note=n_km), kind="token",
                 after=(lambda tok: b2.__setitem__("mn_read", tok)) if u == 3 else None)

        PAD = CONV_WIDTH - 1
        w_in2 = A["w_in_2"]
        glu = at("glu", RD, [P, 8, PAD + T])
        cy = at("conv_y", RA + 24, [P, 8, T])
        yc = Split("yc", RX, RX + 8, 8)
        e2 = sq

        def a_evac(j):
            def evac(bank, tok):
                z = bank[:, :].rearrange("p (c t) -> p c t", c=2)
                if j == 0:
                    b2["pad"] = pool.run(lambda e: e.memset(glu[:, :, 0:PAD], 0.0), *b2["x2"], *b2["xn"])
                t = act.run(lambda e: e.activation(a_buf, z, ACT.Copy, scale=0.5), tok,
                            *((b2["glu"],) if "glu" in b2 else b2["xn"]))
                b2["a"] = t
                return (t,)
            return evac

        a_buf = at("glu_a", 190, [P, 2, T])

        def g_evac(j):
            def evac(bank, tok):
                th = e2[j % 2]
                z = bank[:, :].rearrange("p (c t) -> p c t", c=2)
                t = act.run(lambda e: e.activation(th, z, ACT.Tanh, scale=0.5), tok, *e2_free[j % 2])
                t = dve.run(lambda e: e.scalar_tensor_tensor(glu[:, 2 * j:2 * j + 2, PAD:], th, 1.0, a_buf, ALU.add, ALU.mult),
                            t, b2["a"], *b2["x2"], *b2["xn"])
                e2_free[j % 2] = (t,)
                b2["glu"] = t
                conv_ready.append(t)
                return (b2["a"], t)
            return evac

        conv_ready = []
        TAPS_A_SLOT = 6
        OTHER_PAIR = 1
        ln_tmp = [at("ln_tmp", RD + 4 + 2 * i, [P, 2, T]) for i in range(2)]
        prod = [at("tap_product", RX + i, [P, T]) for i in range(4)]

        def conv_other():
            while len(conv_ready) <= OTHER_PAIR:
                yield
            n, read, t_y = 0, [None] * 4, [None, None]
            for tap in range(CONV_WIDTH):
                for c in range(2):
                    k = 2 * OTHER_PAIR + c
                    w = vec("conv_w", k * CONV_WIDTH + tap)
                    x = glu[:, k, tap:tap + T]
                    if tap == 0:
                        t_y[c] = act.run(lambda e, k=k, x=x, w=w: e.activation(cy[:, k, :], x, ACT.Identity,
                                                                               bias=vec("conv_b", k), scale=w),
                                         conv_ready[OTHER_PAIR], b2["pad"], b2["mn_read"])
                    else:
                        o = prod[n % 4]
                        t = act.run(lambda e, o=o, x=x, w=w: e.activation(o, x, ACT.Copy, scale=w), *([read[n % 4]] if read[n % 4] else [b2["rx_free"]]))
                        t_y[c] = read[n % 4] = pool.run(lambda e, k=k, o=o: e.tensor_tensor(cy[:, k, :], cy[:, k, :], o, ALU.add), t, t_y[c])
                        n += 1
                if tap % 2:
                    yield
            b2["conv_other"] = t_y

        def conv():
            n = 0
            for j in (j for j in range(4) if j != OTHER_PAIR):
                while len(conv_ready) <= j:
                    yield
                last_t = [None, None]
                for c in range(2):
                    k = 2 * j + c
                    last_t[c] = act.run(lambda e, k=k: e.activation(cy[:, k, :], glu[:, k, 0:T], ACT.Identity,
                                                                    bias=vec("conv_b", k), scale=vec("conv_w", k * CONV_WIDTH)),
                                        conv_ready[j], b2["pad"], b2["mn_read"])
                for tap in range(1, CONV_WIDTH):
                    for c in range(2):
                        k = 2 * j + c
                        last_t[c] = dve.run(lambda e, k=k, tap=tap: e.scalar_tensor_tensor(
                            cy[:, k, :], glu[:, k, tap:tap + T], vec("conv_w", k * CONV_WIDTH + tap), cy[:, k, :],
                            ALU.mult, ALU.add), last_t[c])
                        n += 1
                        if n % TAPS_A_SLOT == 0:
                            yield
                b2["conv"] = last_t[0], last_t[1]
            while "conv_other" not in b2:
                yield
            by_t = cy.rearrange("p k t -> p t k")
            t = dve.run(lambda e: e.tensor_reduce(sumsq, by_t, AX.X, ALU.add), *b2["conv"], *b2["conv_other"], last(pe))
            yield
            t = column_sum(sumsq, TB, t)
            yield
            mean = TB[:, 0:T].unsqueeze(1).broadcast_to([P, 4, T])
            for g in range(2):
                t_c = dve.run(lambda e, g=g: e.scalar_tensor_tensor(cy[:, 4 * g:4 * g + 4, :], mean, -1.0 / D_CONV,
                                                                    cy[:, 4 * g:4 * g + 4, :], ALU.mult, ALU.add), t)
            give(TB, t_c)
            sqv = glu[:, :, 0:T]
            yield
            t = act.run(lambda e: e.activation(sqv, cy, ACT.Square), t_c)
            yield
            by_t2 = sqv.rearrange("p k t -> p t k")
            t = dve.run(lambda e: e.tensor_reduce(sumsq, by_t2, AX.X, ALU.add), t, last(pe))
            b2["glu_read"] = (t,)
            yield
            t = column_sum(sumsq, TB, t)
            yield
            t = inverse_std(t, TB, D_CONV)
            r = rstd.unsqueeze(1).broadcast_to([P, 4, T])
            for g in range(2):
                t_g = dve.run(lambda e, g=g: e.tensor_tensor(cy[:, 4 * g:4 * g + 4, :], cy[:, 4 * g:4 * g + 4, :], r, ALU.mult), t)
            yield
            ln_free = [b2["glu_read"]] * 2

            def gain_and_tanh(j):
                for k in (2 * j, 2 * j + 1):
                    t = act.run(lambda e, k=k: e.activation(cy[:, k, :], cy[:, k, :], ACT.Identity, bias=vec("ln_b", k),
                                                            scale=vec("ln_g", k)), t_g)
                th, v = ln_tmp[j % 2], cy[:, 2 * j:2 * j + 2, :]
                return act.run(lambda e: e.activation(th, v, ACT.Tanh, scale=0.5), t, *ln_free[j % 2])

            def silu(j, t):
                th, v = ln_tmp[j % 2], cy[:, 2 * j:2 * j + 2, :]
                t = dve.run(lambda e: e.scalar_tensor_tensor(v, th, 1.0, v, ALU.add, ALU.mult), t)
                ln_free[j % 2] = b2["glu_read"] = (t,)
                return t

            t_th = [gain_and_tanh(j) for j in (0, 1)]
            for first in (0, 2):
                yield
                t_v = [silu(first + i, t_th[i]) for i in range(2)]
                if first == 0:
                    t_th = [gain_and_tanh(j) for j in (2, 3)]
                for i in range(2):
                    j = first + i
                    b2["cy_read"] = yc.make(2 * j, 2 * j + 2, cy[:, 2 * j:2 * j + 2, :], t_v[i], b2["rx_free"])

        g_conv = [None]

        def start_conv(_):
            b2["rx_free"] = last(pe)
            g_conv[0] = spawn(conv())
            spawn(conv_other())

        for j in range(4):
            unit(w_in2, rows, C2_A + j * UNIT, xn, a_evac(j), before=(lambda: finish(g_norms[0])) if j == 0 else None)
            unit(w_in2, rows, C2_G + j * UNIT, xn, g_evac(j), after=start_conv if j == 0 else None)

        q2 = at("q2", RA, [P, 8, T])
        k2 = at("k2", RA + 8, [P, 8, T])
        v2 = at("v2", RA + 16, [P, 2, D_ATTN])
        n_q2, n_k2, n_v2 = [], [], []

        def to_a(dst, note):
            def evac(bank, tok):
                src = bank[:, :].rearrange("p (c t) -> p c t", c=2)
                t = act.run(lambda e: e.copy(dst, src), tok, b2["mn_read"])
                note.append(t)
                return (t,)
            return evac

        for u in range(4):
            unit(w_in2, rows, C2_Q + u * UNIT, xn, to_a(q2[:, 2 * u:2 * u + 2, :], n_q2))
        for u in range(4):
            unit(w_in2, rows, C2_K + u * UNIT, xn, to_a(k2[:, 2 * u:2 * u + 2, :], n_k2))
        for u in range(4):
            unit(w_in2, rows, C2_V + u * UNIT, xn, to_a(v2[:, :, u * UNIT:(u + 1) * UNIT], n_v2), kind="token",
                 after=(lambda tok: spawn(attention2())) if u == 1 else None)

        SC2 = A_DIM ** -0.5
        spare = 199.5 + 264 * 4 / KB
        bias = [at("bias", 192, [P, T + P]), at("bias", spare, [P, T + P])]
        s2 = [at("scores2", 190, [P, T + P]), at("scores2", spare + 1.5, [P, T + P])]
        pt2 = [at("pT2", 193.5, [P, T + P]), at("pT2", spare + 3, [P, T + P])]
        s_mem = at("scores_mem", 190, [P, 2 * T])
        pt_mem = at("pT_mem", 193.5, [P, 2 * T])
        d_bias = [[sem(f"d_bias{i}"), 0] for i in range(2)]
        bias_free, s2_free, pt2_free = [(), ()], [(), ()], [(), ()]
        head2_done = [None] * A_HEADS

        def head2(hd):
            ch, r, b = hd // 2, 64 * (hd % 2), hd % 2
            st = stats[:, 16 * b:16 * b + 16]
            mx, sm = st[:, 0:2], st[:, 2:4]
            B, S, pt = bias[b], s2[b], pt2[b]
            parts = (slice(0, T), slice(T, T + P))
            t_b = pool.dma(B, A["rel_bias"][hd], d_bias[b], *bias_free[b], b2["glu"])
            pool.run(lambda e: e.memset(B[0:64, T - CHUNK:T], NEG), t_b)
            t_m = pool.run(lambda e: e.memset(B[0:64, T + P - CHUNK:T + P], NEG))
            yield

            def score(e):
                kk = slice(r, r + 64)
                e.matmul(SA[:, 0:T], q2[kk, ch, P:T], k2[kk, ch, :], start=True, stop=True)
                return e.matmul(SA[:, T:T + P], q2[kk, ch, 0:P], k2[kk, ch, 0:P], start=True, stop=True)
            t_s = pe.run(score, n_q2[-1], n_k2[-1], *take(SA))
            t = dve.run(lambda e: e.scalar_tensor_tensor(S, SA[:, 0:T + P], SC2, B, ALU.mult, ALU.add), t_s, t_m,
                        *s2_free[b], b2["glu"])
            give(SA, t)
            bias_free[b] = (t,)
            dve.run(lambda e: e.tensor_reduce(mx[:, 0:1], S[:, parts[0]], AX.X, ALU.max), t)
            t = dve.run(lambda e: e.tensor_reduce(mx[:, 1:2], S[:, parts[1]], AX.X, ALU.max))
            t = dve.run(lambda e: e.tensor_scalar(mx, mx, -1.0, None, ALU.mult), t)
            yield
            for i in range(2):
                t_e = act.run(lambda e, v=S[:, parts[i]], i=i: e.activation(v, v, ACT.Exp, bias=mx[:, i:i + 1],
                                                                            accum_out=sm[:, i:i + 1]), t)
            yield
            t = dve.run(lambda e: e.reciprocal(sm, sm), t_e)
            for i in range(2):
                t_p = dve.run(lambda e, v=S[:, parts[i]], i=i: e.tensor_scalar(v, v, sm[:, i:i + 1], None, ALU.mult), t)
            yield

            def flip(e):
                e.transpose(TA[:, 0:P], S[:, 256:384], ident)
                e.transpose(TA[:, P:2 * P], S[:, 0:P], ident)
                return e.transpose(TA[:, 2 * P:3 * P], S[:, P:T], ident)
            t_t = pe.run(flip, t_p, *take(TA))
            s2_free[b] = (t_t,)
            t_pt = act.run(lambda e: e.copy(pt, TA[:, 0:T + P]), t_t, *pt2_free[b])
            give(TA, t_pt)
            yield

            def values(e):
                c = slice(hd * A_DIM, (hd + 1) * A_DIM)
                e.matmul(OB[r:r + 64, 0:T], v2[:, 0, c], pt[:, 0:T], start=True, stop=False, skip_group_check=True)
                return e.matmul(OB[r:r + 64, P:T], v2[:, 1, c], pt[:, T:], start=False, stop=True, skip_group_check=True)
            t_v = pe.run(values, t_pt, n_v2[-1], *take(OB))
            pt2_free[b] = (t_v,)
            t_o = act.run(lambda e: e.copy(q2[r:r + 64, ch, :], OB[r:r + 64, 0:T]), t_v)
            give(OB, t_o)
            head2_done[hd] = t_o

        def attention2():
            for hd in range(A_HEADS):
                next(spawn(head2(hd)))
                for _ in range(1 + hd % 2):
                    yield

        m2 = at("merged2", RD, [P, KD, T])
        gtmp = [at("gate_tmp", 184 + 2 * i, [P, 2, T]) for i in range(2)]
        m2_split = Split("merged2", RA, RX, KD)
        n_m2 = {}

        def gate_evac2(br, c):
            def evac(bank, tok):
                th = gtmp[c % 2]
                for i in range(2):
                    t = act.run(lambda e, i=i: e.activation(th[:, i, :], bank[:, i * T:(i + 1) * T], ACT.Tanh,
                                                            bias=vec("gate_b", 16 * br + 2 * c + i), scale=0.5),
                                tok, *t_half, *e2_free[c % 2])
                n_m2["g", br, c] = t
                return (t,)
            return evac

        def y_evac2(br, c):
            def evac(bank, tok):
                th = gtmp[c % 2]
                m = m2[:, 2 * c:2 * c + 2, :]
                z = bank[:, :].rearrange("p (c t) -> p c t", c=2)
                tg = n_m2["g", br, c]
                if br == 0:
                    t_z = t = dve.run(lambda e: e.scalar_tensor_tensor(m, th, 1.0, z, ALU.add, ALU.mult), tok, tg, *b2["glu_read"])
                else:
                    t_z = dve.run(lambda e: e.scalar_tensor_tensor(th, th, 1.0, z, ALU.add, ALU.mult), tok, tg)
                    t = dve.run(lambda e: e.scalar_tensor_tensor(m, m, 0.5 if br == 1 else 1.0, th, ALU.mult, ALU.add), t_z,
                                n_m2["m", br - 1, c])
                e2_free[c % 2] = (t,)
                n_m2["m", br, c] = t
                if br == 2:
                    m2_split.make(2 * c, 2 * c + 2, m, t, *ao.made[7], *mo.made[7], b2["ao_read"])
                return (t_z,)
            return evac

        def branch(br, w, moving, first_before, last_after):
            for c in range(9):
                if c < 8:
                    unit(w_in2, rows, C2_GATES + br * D + c * UNIT, xn, gate_evac2(br, c))
                if c > 0:
                    unit(w, (0, 1024), (c - 1) * UNIT, moving, y_evac2(br, c - 1), before=first_before if c == 1 else None,
                         after=last_after if c == 8 else None)

        def conv_ready_for_use():
            finish(g_conv[0])

        branch(0, A["w_conv_out"], yc, conv_ready_for_use, lambda tok: b2.__setitem__("yc_read", tok))

        qm = at("q_mem", RA + 8, [P, 8, T])
        n_qm = []
        SCM = M_DIM ** -0.5

        def heads2_done():
            while head2_done[-1] is None:
                advance()

        def qm_evac(u):
            def evac(bank, tok):
                src = bank[:, :].rearrange("p (c t) -> p c t", c=2)
                t = act.run(lambda e: e.copy(qm[:, 2 * u:2 * u + 2, :], src), tok, head2_done[-1])
                n_qm.append(t)
                return (t,)
            return evac

        ao = Split("attn_out", RX, RX + 8, 8)
        mo = Split("mem_out", RA + 16, RA + 24, 8)

        def headm(m):
            yield
            c0 = 2 * m
            st = stats[:, 32 + 8 * (m % 2):40 + 8 * (m % 2)]
            mx, sm = st[:, 0:2], st[:, 2:4]
            S, pt = s_mem, pt_mem

            def score(e):
                for qt in range(2):
                    for i in range(2):
                        x = e.matmul(SA[:, qt * T:(qt + 1) * T], qm[:, c0 + i, qt * P:(qt + 1) * P], k_mem[:, c0 + i, :],
                                     start=i == 0, stop=i == 1)
                return x
            t_s = pe.run(score, n_qm[m], *n_km[0:4], *take(SA))
            v3 = SA[:, :].rearrange("p (m n) -> p m n", m=2)
            t = dve.run(lambda e: e.tensor_reduce(mx, v3, AX.X, ALU.max), t_s)
            t = dve.run(lambda e: e.tensor_scalar(mx, mx, -SCM, None, ALU.mult), t)
            for i in range(2):
                t_e = act.run(lambda e, i=i: e.activation(S[:, i * T:(i + 1) * T], SA[:, i * T:(i + 1) * T], ACT.Exp,
                                                          bias=mx[:, i:i + 1], scale=SCM, accum_out=sm[:, i:i + 1]),
                              t, *s2_free[0])
            give(SA, t_e)
            t = dve.run(lambda e: e.reciprocal(sm, sm), t_e)
            for i in range(2):
                t_p = dve.run(lambda e, i=i: e.tensor_scalar(S[:, i * T:(i + 1) * T], S[:, i * T:(i + 1) * T], sm[:, i:i + 1],
                                                             None, ALU.mult), t)
            yield

            def flip(e):
                for kt in range(2):
                    for qt in range(2):
                        x = e.transpose(TA[:, kt * T + qt * P:kt * T + (qt + 1) * P], S[:, qt * T + kt * P:qt * T + (kt + 1) * P], ident)
                return x
            t_t = pe.run(flip, t_p, *take(TA))
            s2_free[0] = (t_t,)
            t = act.run(lambda e: e.copy(pt, TA[:, :]), t_t, *pt2_free[0])
            give(TA, t)
            yield

            def values(e):
                for i in range(2):
                    for kt in range(2):
                        x = e.matmul(OB[:, i * T:(i + 1) * T], v_mem[:, kt, (c0 + i) * P:(c0 + i + 1) * P],
                                     pt[:, kt * T:(kt + 1) * T], start=kt == 0, stop=kt == 1)
                return x
            t_v = pe.run(values, t, *n_km[4:8], *take(OB))
            pt2_free[0] = (t_v,)
            v = OB[:, :].rearrange("p (c t) -> p c t", c=2)
            t_o = act.run(lambda e: e.copy(qm[:, c0:c0 + 2, :], v), t_v)
            give(OB, t_o)
            mo.make(c0, c0 + 2, qm[:, c0:c0 + 2, :], t_o, head2_done[-1], *b2["cy_read"])

        def mem_heads():
            for m in range(M_HEADS):
                yield from headm(m)

        def split_ao(tok):
            for c in range(4):
                ao.make(2 * c, 2 * c + 2, q2[:, 2 * c:2 * c + 2, :], head2_done[4 * c + 1], head2_done[4 * c + 3], b2["yc_read"])
            g_memh.append(spawn(mem_heads()))

        g_memh = []
        for u in range(4):
            unit(w_in2, rows, C2_QM + u * UNIT, xn, qm_evac(u), before=heads2_done if u == 0 else None,
                 after=split_ao if u == 3 else None)
        branch(1, A["w_attn_out"], ao, None, lambda tok: b2.__setitem__("ao_read", tok))

        def mem_ready():
            finish(g_memh[0])

        branch(2, A["w_mem_out"], mo, mem_ready, None)

        hres = at("h_res", RD, [P, KD, T])
        x2r = [at("x2_again", RC + 12 + 2 * i, [P, 2, T]) for i in range(2)]
        n_h, h_tokens, t_x2r = [], [], {}
        d_x2r = [[sem(f"d_x2r{i}"), 0] for i in range(2)]

        def load_x2(c):
            def f():
                t_x2r[c] = act.dma(x2r[c % 2], x2_dram[:, 2 * c:2 * c + 2, :], d_x2r[c % 2], *b2["x2"],
                                   *([n_h[c - 2]] if c >= 2 else [last(pe)]))
            return f

        def wo_evac(c):
            def evac(bank, tok):
                z = bank[:, :].rearrange("p (c t) -> p c t", c=2)
                t = dve.run(lambda e: e.scalar_tensor_tensor(hres[:, 2 * c:2 * c + 2, :], z, 0.5, x2r[c % 2], ALU.mult, ALU.add),
                            tok, t_x2r[c], *m2_split.made[15])
                n_h.append(t)
                h_tokens.append((t,))
                return (t,)
            return evac

        hn = Split("hn", RB, RB + 16, KD)
        g_gain, g_ffn, t_ffn_rstd = [None], [None], []

        def gained(src, tokens, gain, split, *split_free):
            for j in range(KD // 2):
                while len(tokens) <= j:
                    yield
                for k in (2 * j, 2 * j + 1):
                    hi, lo, x, g = split.hi[:, k, :], split.lo[:, k, :], src[:, k, :], vec(gain, k)
                    t_hi = act.run(lambda e, hi=hi, x=x, g=g: e.activation(hi, x, ACT.Copy, scale=g), *tokens[j], *split_free)
                    t_lo = dve.run(lambda e, hi=hi, lo=lo, x=x, g=g: e.scalar_tensor_tensor(
                        lo, x, g, hi.bitcast(F32), ALU.mult, ALU.subtract), t_hi, *tokens[j], *split_free)
                    split.made[k] = (t_hi, t_lo)

        def ffn_rstd():
            t_ffn_rstd.append((yield from mean_square(hres, h_tokens)))

        def after_wo(c):
            def f(tok):
                if c == 0:
                    preload_sqrt()
                    g_gain[0] = spawn(gained(hres, h_tokens, "ffn_norm", hn, tok))
                    g_ffn[0] = spawn(ffn_rstd())
                b2["a_free"] = tok
            return f

        for c in range(8):
            unit(A["w_o"], rows, c * UNIT, m2_split, wo_evac(c), before=load_x2(c), after=after_wo(c))

        HALF = D_FF // 2
        HK = HALF // P
        gated = Split("gated", RA, RA + 22, HK)
        fv = [at("ffn_val", RX + 4 * i, [P, 2, T]) for i in range(2)]
        fg = [at("ffn_gate", RX + 2 + 4 * i, [P, 2, T]) for i in range(2)]
        ft = [at("ffn_tanh", RX + 8 + 2 * i, [P, 2, T]) for i in range(2)]
        fz = [at("ffn_normed", RX + 12 + 2 * i, [P, 2, T]) for i in range(2)]
        fz_free = [(), ()]
        f_free = {0: (), 1: ()}
        gated_free = [None]
        ffn = {}

        def conv3(dst, which, bank, tok, k0, *free):
            if not t_ffn_rstd:
                finish(g_ffn[0])
            w = lambda i, tap: vec("ffn_w", (k0 + i) * FFN_TAPS + tap)
            zn = fz[which]
            z = bank[:, :].rearrange("p (c t) -> p c t", c=2)
            r = rstd.unsqueeze(1).broadcast_to([P, 2, T])
            t_z = dve.run(lambda e: e.tensor_tensor(zn, z, r, ALU.mult), tok, *t_ffn_rstd, b2["a_free"], *fz_free[which])
            for i in range(2):
                t = act.run(lambda e, i=i: e.activation(dst[:, i, :], zn[:, i, :], ACT.Identity, bias=vec("ffn_b", k0 + i),
                                                        scale=w(i, 2)), t_z, *free)
            last_t = [t, t]
            for back in (1, 2):
                for i in range(2):
                    last_t[i] = dve.run(lambda e, i=i, b=back: e.scalar_tensor_tensor(
                        dst[:, i, b:], zn[:, i, :T - b], w(i, 2 - b), dst[:, i, b:], ALU.mult, ALU.add), last_t[i])
            fz_free[which] = tuple(last_t)
            return t_z, last_t

        def val_evac(half, j):
            def evac(bank, tok):
                t_z, done = conv3(fv[j % 2], 0, bank, tok, half * HK + 2 * j, *f_free[j % 2])
                ffn["v"] = done
                return (t_z,)
            return evac

        def gate_value(j, gate_done, val_done):
            b = j % 2
            t = act.run(lambda e: e.activation(ft[b], fg[b], ACT.Tanh, scale=0.5), *gate_done, *f_free[b])
            yield
            t = dve.run(lambda e: e.scalar_tensor_tensor(fg[b], ft[b], 1.0, fg[b], ALU.add, ALU.mult), t)
            t = dve.run(lambda e: e.tensor_tensor(fg[b], fg[b], fv[b], ALU.mult), t, *val_done)
            yield
            f_free[b] = gated.make(2 * j, 2 * j + 2, fg[b], t, gated_free[0], b2["a_free"])

        def gate_evac(half, j):
            def evac(bank, tok):
                b = j % 2
                t_z, done = conv3(fg[b], 1, bank, tok, D_FF // P + half * HK + 2 * j, *f_free[b])
                ffn["gate"] = spawn(gate_value(j, done, ffn["v"]))
                return (t_z,)
            return evac

        def down_evac(half, c):
            def evac(bank, tok):
                z = bank[:, :].rearrange("p (c t) -> p c t", c=2)
                m = hres[:, 2 * c:2 * c + 2, :]
                t = dve.run(lambda e: e.scalar_tensor_tensor(m, z, 0.5, m, ALU.mult, ALU.add), tok, n_h[c],
                            *([hn.made[15][1]] if half == 0 else []))
                n_h[c] = t
                return (t,)
            return evac

        def ffn_start():
            finish(g_gain[0])
            gated_free[0] = b2["a_free"]

        final_tokens, final = [], []
        g_final = [None]

        def last_norm():
            pairs = KD // 2
            t_g = []
            for j in range(pairs):
                while len(final_tokens) <= j:
                    yield
                s, v = sq[j % 2], hres[:, 2 * j:2 * j + 2, :]
                t_sq = act.run(lambda e, s=s, v=v: e.activation(s, v, ACT.Square), *final_tokens[j], *sq_read[j % 2])
                if j < pairs - 1:
                    for k in (2 * j, 2 * j + 1):
                        t = act.run(lambda e, k=k: e.activation(hres[:, k, :], hres[:, k, :], ACT.Copy,
                                                                scale=vec("final_norm_2", k)), t_sq)
                    t_g.append(t)
                    for c in range(2):
                        if j == 0 and c == 0:
                            t = dve.run(lambda e, s=s: e.tensor_tensor(sumsq, s[:, 0, :], s[:, 1, :], ALU.add), t_sq, last(pe))
                        elif j > 0:
                            t = dve.run(lambda e, s=s, c=c: e.tensor_tensor(sumsq, sumsq, s[:, c, :], ALU.add), t_sq, t_sum)
                        t_sum = t
                    sq_read[j % 2] = (t_sum,)
                yield
            pe.run(lambda e: e.matmul(TB[:, 0:T], ones, sumsq, start=True, stop=False), t_sum, *take(TB))
            for c in range(2):
                t = pe.run(lambda e, c=c: e.matmul(TB[:, 0:T], ones, s[:, c, :], start=False, stop=c == 1), t_sq)
            t_rstd = inverse_std(t, TB, D)
            r = rstd.unsqueeze(1).broadcast_to([P, 2, T])
            for k in (KD - 2, KD - 1):
                t = dve.run(lambda e, k=k: e.scalar_tensor_tensor(hres[:, k, :], hres[:, k, :], vec("final_norm_2", k), rstd,
                                                                  ALU.mult, ALU.mult), t_rstd)
            final.append((pairs - 1, t))
            for j in range(pairs - 1):
                v = hres[:, 2 * j:2 * j + 2, :]
                q = pool if j % 5 == 0 or j == 3 else dve
                t = q.run(lambda e, v=v: e.tensor_tensor(v, v, r, ALU.mult), t_rstd, t_g[j])
                final.append((j, t))

        def after_down(half, c):
            def f(tok):
                if half == 1:
                    final_tokens.append((n_h[c],))
                    if c == 0:
                        preload_sqrt()
                        g_final[0] = spawn(last_norm())
                elif c == 7:
                    gated_free[0] = tok
            return f

        for half in range(2):
            for j in range(HALF // UNIT):
                unit(A["w_up"], rows, half * HALF + j * UNIT, hn, val_evac(half, j),
                     before=ffn_start if half == 0 and j == 0 else None)
                unit(A["w_up"], rows, D_FF + half * HALF + j * UNIT, hn, gate_evac(half, j))
            for c in range(8):
                unit(A["w_down"], (half * HALF, (half + 1) * HALF), c * UNIT, gated, down_evac(half, c),
                     before=(lambda: finish(ffn["gate"])) if c == 0 else None, after=after_down(half, c))

        drive()

        d_out = [sem("d_out"), 0]
        out_v = chunked(out)
        for j, t in final:
            t_out = sp.dma(out_v[:, 2 * j:2 * j + 2, :], hres[:, 2 * j:2 * j + 2, :], d_out, t)
        sp.wait(t_out)
        sp.wait(*b2["x2"])

        block = ctx.enter_context(nc.Block())

        @block.sync
        def _(e):
            sp.play(e)

        @block.scalar
        def _(e):
            act.play(e)

        @block.vector
        def _(e):
            dve.play(e)

        @block.gpsimd
        def _(e):
            pool.play(e)

        @block.tensor
        def _(e):
            pe.play(e)


def kernel(**inputs):
    import concourse.bacc as bacc
    from concourse.bass_utils import run_bass_kernel_spmd as run

    def layer(name):
        return np.ascontiguousarray(np.asarray(inputs[name])[0])

    def chunks(v):
        return v.reshape(-1, P).T

    def taps(w):
        return w.reshape(w.shape[0], -1, P).transpose(2, 1, 0).reshape(P, -1)

    parts = {
        "norm_w": chunks(layer("norm_w")), "pool_scale": chunks(layer("pool_scale")),
        "b_merge": chunks(layer("b_merge")), "final_norm_w": chunks(np.asarray(inputs["final_norm_w"])),
        "pe_k": layer("cmp_pe_k").T, "pe_v": layer("cmp_pe_v").T,
        "mix_norm": chunks(layer("mix_norm_g_2")), "mem_norm": chunks(layer("mem_norm_g_2")),
        "gate_b": chunks(layer("gate_b_2")), "conv_w": taps(layer("conv_w_2")), "conv_b": chunks(layer("conv_b_2")),
        "ln_g": chunks(layer("conv_ln_g_2")), "ln_b": chunks(layer("conv_ln_b_2")),
        "ffn_norm": chunks(layer("ffn_norm_g_2")), "ffn_w": taps(layer("ffn_conv_w_2")),
        "ffn_b": chunks(layer("ffn_conv_b_2")), "final_norm_2": chunks(np.asarray(inputs["final_norm_g_2"])),
    }
    windows = np.lib.stride_tricks.sliding_window_view(layer("rel_bias_2")[:, ::-1], T, axis=1)
    rows_q = windows[:, MAX_REL - np.arange(T), :]
    rel = np.concatenate([rows_q[:, P:, :], rows_q[:, :P, :P]], axis=2)
    w_gates = layer("w_in")[:, C_GBR:].reshape(KD, P, N_GATES).transpose(1, 0, 2).reshape(P, KD * N_GATES)
    arrays = {
        "vecs": np.concatenate([parts[name] for name, _ in VECS], axis=1), "consts": shape_constants(),
        "x": layer("x").T, "mem": layer("mem_2").T, "rel_bias": rel,
        "w_in": layer("w_in"), "w_gates": w_gates, "pool_mix": layer("pool_mix"), "cmp_w1_k": layer("cmp_w1_k"), "cmp_w2_k": layer("cmp_w2_k"),
        "cmp_w1_v": layer("cmp_w1_v"), "cmp_w2_v": layer("cmp_w2_v"), "w_pool_out": layer("w_pool_out"),
        "w_nsa_out": layer("w_nsa_out"), "w_merge": layer("w_merge"), "w_out": layer("w_out"),
        "w_in_2": layer("w_in_2"), "w_conv_out": layer("w_conv_out_2"), "w_attn_out": layer("w_attn_out_2"),
        "w_mem_kv": layer("w_mem_kv_2"), "w_mem_out": layer("w_mem_out_2"), "w_o": layer("w_o_2"),
        "w_up": layer("w_up_2"), "w_down": layer("w_down_2"),
    }
    arrays = {k: np.ascontiguousarray(v) for k, v in arrays.items()}
    nc = bacc.Bacc("TRN2", target_bir_lowering=False, num_devices=1)
    aps = {k: nc.dram_tensor(k, v.shape, F32, kind="ExternalInput").ap() for k, v in arrays.items()}
    out = nc.dram_tensor("out", (D, T), F32, kind="ExternalOutput").ap()
    two_blocks(nc, aps, out)
    got = run(nc, [arrays], core_ids=[0]).results[0]["out"]
    return np.ascontiguousarray(got.T)[None]
```
